# Optimizing a Trainium2 kernel written in Bass

```python
import math
import jax, jax.numpy as jnp
from jax import lax
import numpy as np

D_MODEL = 1024
BATCH = 1
SEQ = 256
DEPTH = 2

MEM_LEN = 256
DA_HEADS = 8
DA_HEAD_DIM = 64
DA_V_DIM = 2 * DA_HEAD_DIM
DA_WIDTH = DA_HEADS * DA_V_DIM
QK_WIDTH = DA_HEADS * 2 * DA_HEAD_DIM
LAMBDA_INIT_SCALE = 0.1
CONV_WIDTH = 512
CONV_K = 3
MEM_HEADS = 4
MEM_HEAD_DIM = 128
MEM_WIDTH = MEM_HEADS * MEM_HEAD_DIM
N_BRANCH = 3
ROPE_THETA = 10000.0
Q_BLOCK = 128
N_EXPERTS = 16
N_GROUPS = 4
EXPERTS_PER_GROUP = N_EXPERTS // N_GROUPS
TOP_K = 2
D_FF_EXPERT = 512
EXPERT_BLOCK = 128
LN_EPS = 1e-5
RMS_EPS = 1e-5
DEEPNORM_ALPHA = (2 * DEPTH) ** 0.25
DEEPNORM_BETA = (8 * DEPTH) ** -0.25

IN_SIZES = (QK_WIDTH, QK_WIDTH, DA_WIDTH, CONV_WIDTH, CONV_WIDTH, CONV_WIDTH, MEM_WIDTH, N_BRANCH * D_MODEL)
IN_COLS = sum(IN_SIZES)
IN_SPLITS = tuple(sum(IN_SIZES[:i + 1]) for i in range(len(IN_SIZES) - 1))


def layer_norm(x, g, b):
    x32 = x.astype(jnp.float32)
    mu = jnp.mean(x32, axis=-1, keepdims=True)
    var = jnp.mean(jnp.square(x32 - mu), axis=-1, keepdims=True)
    y = (x32 - mu) * lax.rsqrt(var + LN_EPS) * g.astype(jnp.float32) + b.astype(jnp.float32)
    return y.astype(x.dtype)

def rope(t, cos, sin):
    half = t.shape[-1] // 2
    t1, t2 = t[..., :half], t[..., half:]
    cos = cos.astype(t.dtype)
    sin = sin.astype(t.dtype)
    return jnp.concatenate([t1 * cos - t2 * sin, t2 * cos + t1 * sin], axis=-1)

def diff_attention(q, k, v, lam, lam_init, subln_g):
    B, S = q.shape[0], q.shape[1]
    qh = jnp.transpose(q, (0, 2, 3, 1, 4))
    kh = jnp.transpose(k, (0, 2, 3, 1, 4))
    vh = jnp.transpose(v, (0, 2, 1, 3))
    scale = DA_HEAD_DIM ** -0.5
    outs = []
    for blk in range(S // Q_BLOCK):
        s0 = blk * Q_BLOCK
        end = s0 + Q_BLOCK
        qb = qh[:, :, :, s0:end]
        kb = kh[:, :, :, :end]
        sc = jnp.einsum('bhcqd,bhckd->bhcqk', qb, kb).astype(jnp.float32) * scale
        causal = jnp.arange(end)[None, :] <= (s0 + jnp.arange(Q_BLOCK))[:, None]
        sc = jnp.where(causal, sc, -jnp.inf)
        p = jax.nn.softmax(sc, axis=-1)
        a = p[:, :, 0] - lam * p[:, :, 1]
        outs.append(jnp.einsum('bhqk,bhkd->bhqd', a.astype(v.dtype), vh[:, :, :end]))
    o = jnp.concatenate(outs, axis=2).astype(jnp.float32)
    o = o * lax.rsqrt(jnp.mean(jnp.square(o), axis=-1, keepdims=True) + RMS_EPS)
    o = o * subln_g.astype(jnp.float32) * (1.0 - lam_init)
    o = jnp.transpose(o, (0, 2, 1, 3)).astype(v.dtype)
    return o.reshape(B, S, DA_WIDTH)

def short_gated_conv(bg, cg, u, w):
    z = cg * u
    S = z.shape[1]
    zp = jnp.pad(z, ((0, 0), (CONV_K - 1, 0), (0, 0)))
    y = w[0] * zp[:, 0:S]
    for tap in range(1, CONV_K):
        y = y + w[tap] * zp[:, tap:tap + S]
    return bg * y

def memory_attention(qm, mem, w_kv):
    B, S = qm.shape[0], qm.shape[1]
    M = mem.shape[1]
    kv = mem @ w_kv
    km = kv[..., :MEM_WIDTH].reshape(B, M, MEM_HEADS, MEM_HEAD_DIM)
    vm = kv[..., MEM_WIDTH:].reshape(B, M, MEM_HEADS, MEM_HEAD_DIM)
    q = qm.reshape(B, S, MEM_HEADS, MEM_HEAD_DIM)
    sc = jnp.einsum('bshd,bmhd->bhsm', q, km).astype(jnp.float32) * (MEM_HEAD_DIM ** -0.5)
    p = jax.nn.softmax(sc, axis=-1)
    o = jnp.einsum('bhsm,bmhd->bshd', p.astype(vm.dtype), vm)
    return o.reshape(B, S, MEM_WIDTH)

def grouped_moe(x2d, w_router, router_bias, w_gate, w_up, w_down):
    T, D = x2d.shape
    logits = (x2d @ w_router).astype(jnp.float32) + router_bias.astype(jnp.float32)
    scores = jax.nn.softmax(logits, axis=-1)
    grouped = scores.reshape(T, N_GROUPS, EXPERTS_PER_GROUP)
    g_idx = jnp.argmax(jnp.max(grouped, axis=-1), axis=-1)
    in_group = jnp.take_along_axis(grouped, g_idx[:, None, None], axis=1)[:, 0]
    top_vals, top_idx = lax.top_k(in_group, TOP_K)
    experts = g_idx[:, None] * EXPERTS_PER_GROUP + top_idx
    weights = top_vals / jnp.sum(top_vals, axis=-1, keepdims=True)

    A = T * TOP_K
    e_flat = experts.reshape(A).astype(jnp.int32)
    tok_flat = jnp.repeat(jnp.arange(T, dtype=jnp.int32), TOP_K)
    gate_flat = weights.reshape(A).astype(x2d.dtype)
    order = jnp.argsort(e_flat)
    e_sorted = e_flat[order]
    counts = jnp.zeros((N_EXPERTS,), jnp.int32).at[e_flat].add(1)
    start = jnp.cumsum(counts) - counts
    padded = ((counts + EXPERT_BLOCK - 1) // EXPERT_BLOCK) * EXPERT_BLOCK
    pad_end = jnp.cumsum(padded)
    pad_start = pad_end - padded
    dest = pad_start[e_sorted] + (jnp.arange(A, dtype=jnp.int32) - start[e_sorted])
    P = ((A + EXPERT_BLOCK - 1) // EXPERT_BLOCK) * EXPERT_BLOCK + N_EXPERTS * EXPERT_BLOCK
    n_blocks = P // EXPERT_BLOCK
    buf_tok = jnp.full((P,), T, jnp.int32).at[dest].set(tok_flat[order])
    buf_gate = jnp.zeros((P,), x2d.dtype).at[dest].set(gate_flat[order])
    blk_start = jnp.arange(n_blocks, dtype=jnp.int32) * EXPERT_BLOCK
    blk_expert = jnp.minimum(jnp.searchsorted(pad_end, blk_start, side='right'), N_EXPERTS - 1).astype(jnp.int32)
    x_pad = jnp.concatenate([x2d, jnp.zeros((1, D), x2d.dtype)], axis=0)
    xb = x_pad[buf_tok].reshape(n_blocks, EXPERT_BLOCK, D)

    def expert_block(args):
        xblk, e = args
        h = jax.nn.silu(xblk @ w_gate[e]) * (xblk @ w_up[e])
        return h @ w_down[e]

    yb = lax.map(expert_block, (xb, blk_expert))
    y = yb.reshape(P, D) * buf_gate[:, None]
    return jax.ops.segment_sum(y, buf_tok, num_segments=T + 1)[:T]

def first_inputs(seed: int = 0) -> dict:
    key = jax.random.key(seed)
    ks = jax.random.split(key, 26)
    f32 = jnp.float32

    def nrm(k, shape, fan_in, scale=1.0):
        return jax.random.normal(k, shape, f32) * (scale * fan_in ** -0.5)

    x = jax.random.normal(ks[0], (BATCH, SEQ, D_MODEL), f32)
    mem = jax.random.normal(ks[1], (BATCH, MEM_LEN, D_MODEL), f32)
    positions = (jax.random.randint(ks[2], (BATCH, 1), 0, 4096, jnp.int32)
                 + jnp.arange(SEQ, dtype=jnp.int32)[None, :])
    col_scale = jnp.concatenate([
        jnp.ones((2 * QK_WIDTH,), f32),
        jnp.full((DA_WIDTH,), DEEPNORM_BETA, f32),
        jnp.ones((IN_COLS - 2 * QK_WIDTH - DA_WIDTH,), f32)])
    w_in = nrm(ks[3], (DEPTH, D_MODEL, IN_COLS), D_MODEL) * col_scale
    lambda_q1 = LAMBDA_INIT_SCALE * jax.random.normal(ks[4], (DEPTH, DA_HEAD_DIM), f32)
    lambda_k1 = LAMBDA_INIT_SCALE * jax.random.normal(ks[5], (DEPTH, DA_HEAD_DIM), f32)
    lambda_q2 = LAMBDA_INIT_SCALE * jax.random.normal(ks[6], (DEPTH, DA_HEAD_DIM), f32)
    lambda_k2 = LAMBDA_INIT_SCALE * jax.random.normal(ks[7], (DEPTH, DA_HEAD_DIM), f32)
    diff_subln_g = 1.0 + 0.02 * jax.random.normal(ks[8], (DEPTH, DA_V_DIM), f32)
    conv_w = nrm(ks[9], (DEPTH, CONV_K, CONV_WIDTH), CONV_K)
    w_mem_kv = nrm(ks[10], (DEPTH, D_MODEL, 2 * MEM_WIDTH), D_MODEL)
    w_br_attn = nrm(ks[11], (DEPTH, DA_WIDTH, D_MODEL), DA_WIDTH, DEEPNORM_BETA)
    w_br_conv = nrm(ks[12], (DEPTH, CONV_WIDTH, D_MODEL), CONV_WIDTH, DEEPNORM_BETA)
    w_br_mem = nrm(ks[13], (DEPTH, MEM_WIDTH, D_MODEL), MEM_WIDTH, DEEPNORM_BETA)
    w_out = nrm(ks[14], (DEPTH, D_MODEL, D_MODEL), D_MODEL, DEEPNORM_BETA)
    ln1_g = 1.0 + 0.02 * jax.random.normal(ks[15], (DEPTH, D_MODEL), f32)
    ln1_b = 0.02 * jax.random.normal(ks[16], (DEPTH, D_MODEL), f32)
    ln2_g = 1.0 + 0.02 * jax.random.normal(ks[17], (DEPTH, D_MODEL), f32)
    ln2_b = 0.02 * jax.random.normal(ks[18], (DEPTH, D_MODEL), f32)
    w_router = nrm(ks[19], (D_MODEL, N_EXPERTS), D_MODEL)
    router_bias = 0.01 * jax.random.normal(ks[20], (N_EXPERTS,), f32)
    w_exp_gate = nrm(ks[21], (DEPTH, N_EXPERTS, D_MODEL, D_FF_EXPERT), D_MODEL, DEEPNORM_BETA)
    w_exp_up = nrm(ks[22], (DEPTH, N_EXPERTS, D_MODEL, D_FF_EXPERT), D_MODEL, DEEPNORM_BETA)
    w_exp_down = nrm(ks[23], (DEPTH, N_EXPERTS, D_FF_EXPERT, D_MODEL), D_FF_EXPERT, DEEPNORM_BETA)
    return {'x': x, 'mem': mem, 'positions': positions, 'w_in': w_in,
            'lambda_q1': lambda_q1, 'lambda_k1': lambda_k1, 'lambda_q2': lambda_q2, 'lambda_k2': lambda_k2,
            'diff_subln_g': diff_subln_g, 'conv_w': conv_w, 'w_mem_kv': w_mem_kv,
            'w_br_attn': w_br_attn, 'w_br_conv': w_br_conv, 'w_br_mem': w_br_mem, 'w_out': w_out,
            'ln1_g': ln1_g, 'ln1_b': ln1_b, 'ln2_g': ln2_g, 'ln2_b': ln2_b,
            'w_router': w_router, 'router_bias': router_bias,
            'w_exp_gate': w_exp_gate, 'w_exp_up': w_exp_up, 'w_exp_down': w_exp_down}

def first_block(x, mem, positions, w_in, lambda_q1, lambda_k1, lambda_q2, lambda_k2, diff_subln_g,
              conv_w, w_mem_kv, w_br_attn, w_br_conv, w_br_mem, w_out,
              ln1_g, ln1_b, ln2_g, ln2_b, w_router, router_bias,
              w_exp_gate, w_exp_up, w_exp_down):
    B, S, D = x.shape
    inv_freq = ROPE_THETA ** (-jnp.arange(0, DA_HEAD_DIM, 2, dtype=jnp.float32) / DA_HEAD_DIM)
    ang = positions.astype(jnp.float32)[..., None] * inv_freq
    cos = jnp.cos(ang)[:, :, None, :]
    sin = jnp.sin(ang)[:, :, None, :]

    for l in range(DEPTH):
        lam_init = 0.8 - 0.6 * math.exp(-0.3 * l)
        proj = x @ w_in[l]
        q, k, v, cb, cc, cu, qm, gates = jnp.split(proj, IN_SIZES and IN_SPLITS, axis=-1)

        q = rope(q.reshape(B, S, DA_HEADS * 2, DA_HEAD_DIM), cos, sin).reshape(B, S, DA_HEADS, 2, DA_HEAD_DIM)
        k = rope(k.reshape(B, S, DA_HEADS * 2, DA_HEAD_DIM), cos, sin).reshape(B, S, DA_HEADS, 2, DA_HEAD_DIM)
        v = v.reshape(B, S, DA_HEADS, DA_V_DIM)
        lam = (jnp.exp(jnp.sum(lambda_q1[l].astype(jnp.float32) * lambda_k1[l].astype(jnp.float32)))
               - jnp.exp(jnp.sum(lambda_q2[l].astype(jnp.float32) * lambda_k2[l].astype(jnp.float32)))
               + lam_init)
        y_attn = diff_attention(q, k, v, lam, lam_init, diff_subln_g[l])

        y_conv = short_gated_conv(cb, cc, cu, conv_w[l])

        y_mem = memory_attention(qm, mem, w_mem_kv[l])

        g = jax.nn.sigmoid(gates.reshape(B, S, N_BRANCH, D))
        merged = (g[:, :, 0] * (y_attn @ w_br_attn[l])
                  + g[:, :, 1] * (y_conv @ w_br_conv[l])
                  + g[:, :, 2] * (y_mem @ w_br_mem[l]))
        mix = merged @ w_out[l]
        x = layer_norm(DEEPNORM_ALPHA * x + mix, ln1_g[l], ln1_b[l])

        f = grouped_moe(x.reshape(B * S, D), w_router, router_bias,
                        w_exp_gate[l], w_exp_up[l], w_exp_down[l]).reshape(B, S, D)
        x = layer_norm(DEEPNORM_ALPHA * x + f, ln2_g[l], ln2_b[l])
    return x


CTX_LEN = 256
GRID_W = 64
HEAD_DIM = 64
A_Q_HEADS = 6
A_KV_HEADS = 2
F_GROUPS = 4
F_GROUP_CH = 64
C_Q_HEADS = 6
C_KV_HEADS = 2
WINDOW = 128
AXIS_ROT = HEAD_DIM // 2
D_FF = -(-8 * D_MODEL // (3 * 256)) * 256
NORM_EPS = 1e-6
NEG_INF = -1e30

Q_A_W = A_Q_HEADS * HEAD_DIM
KV_A_W = A_KV_HEADS * HEAD_DIM
F_W = F_GROUPS * F_GROUP_CH
Q_C_W = C_Q_HEADS * HEAD_DIM
KV_C_W = C_KV_HEADS * HEAD_DIM
IN_WIDTH = Q_A_W + 2 * KV_A_W + F_W + Q_C_W + 2 * KV_C_W
MIX_WIDTH = Q_A_W + F_W + Q_C_W


def rms_norm(x, g):
    xf = x.astype(jnp.float32)
    y = xf * lax.rsqrt(jnp.mean(xf * xf, axis=-1, keepdims=True) + NORM_EPS)
    return (y * g.astype(jnp.float32)).astype(x.dtype)

def adaln(cond, w_ada, b_ada):
    m = jax.nn.silu(cond) @ w_ada + b_ada
    return jnp.split(m, 6, axis=-1)

def axial_rope_tables(n_tokens):
    rows = n_tokens // GRID_W
    row = jnp.repeat(jnp.arange(rows, dtype=jnp.float32), GRID_W)
    col = jnp.tile(jnp.arange(GRID_W, dtype=jnp.float32), rows)
    inv_freq = ROPE_THETA ** (-jnp.arange(0, AXIS_ROT, 2, dtype=jnp.float32) / AXIS_ROT)
    ang = jnp.concatenate([row[:, None] * inv_freq, col[:, None] * inv_freq], axis=-1)
    return jnp.cos(ang), jnp.sin(ang)

def apply_rope(x, cos, sin):
    xf = x.astype(jnp.float32)
    half = HEAD_DIM // 2
    x1, x2 = xf[..., :half], xf[..., half:]
    c = cos[None, :, None, :]
    s = sin[None, :, None, :]
    return jnp.concatenate([x1 * c - x2 * s, x2 * c + x1 * s], axis=-1).astype(x.dtype)

def gqa_logits(q, k):
    b, lq, h, dh = q.shape
    kvh = k.shape[2]
    qg = q.reshape(b, lq, kvh, h // kvh, dh)
    return jnp.einsum('bqhgd,bkhd->bhgqk', qg, k, preferred_element_type=jnp.float32) * (dh ** -0.5)

def gqa_combine(p, v):
    o = jnp.einsum('bhgqk,bkhd->bqhgd', p.astype(v.dtype), v)
    return o.reshape(o.shape[0], o.shape[1], -1)

def sink_logits(sink, like):
    kvh, g = like.shape[1], like.shape[2]
    return jnp.broadcast_to(sink.astype(jnp.float32).reshape(1, kvh, g, 1, 1), like.shape[:-1] + (1,))

def dense_attention(q, k, v, sink=None):
    s = gqa_logits(q, k)
    if sink is None:
        return gqa_combine(jax.nn.softmax(s, axis=-1), v)
    s = jnp.concatenate([s, sink_logits(sink, s)], axis=-1)
    p = jax.nn.softmax(s, axis=-1)[..., :-1]
    return gqa_combine(p, v)

def global_attention(q, k, v, k_ctx, v_ctx):
    b, s, h, dh = q.shape
    nb = s // Q_BLOCK
    k_all = jnp.concatenate([k_ctx, k], axis=1)
    v_all = jnp.concatenate([v_ctx, v], axis=1)
    qb = jnp.moveaxis(q.reshape(b, nb, Q_BLOCK, h, dh), 1, 0)
    ob = lax.map(lambda qi: dense_attention(qi, k_all, v_all), qb)
    return jnp.moveaxis(ob, 0, 1).reshape(b, s, h * dh)

def window_attention(q, k, v, k_ctx, v_ctx, sink):
    b, s, h, dh = q.shape
    nb = s // Q_BLOCK
    band = Q_BLOCK + 2 * WINDOW
    n_ctx = k_ctx.shape[1]
    pad = ((0, 0), (WINDOW, WINDOW), (0, 0), (0, 0))
    kp = jnp.pad(k, pad)
    vp = jnp.pad(v, pad)
    qb = jnp.moveaxis(q.reshape(b, nb, Q_BLOCK, h, dh), 1, 0)
    qi_idx = jnp.arange(Q_BLOCK)[:, None]
    kj = jnp.arange(band)[None, :]
    in_window = jnp.abs(kj - WINDOW - qi_idx) <= WINDOW

    def one_block(args):
        qi, n = args
        start = n * Q_BLOCK
        kb = lax.dynamic_slice_in_dim(kp, start, band, axis=1)
        vb = lax.dynamic_slice_in_dim(vp, start, band, axis=1)
        kpos = start - WINDOW + kj
        valid = in_window & (kpos >= 0) & (kpos < s)
        s_loc = jnp.where(valid, gqa_logits(qi, kb), NEG_INF)
        s_ctx = gqa_logits(qi, k_ctx)
        logits = jnp.concatenate([s_loc, s_ctx, sink_logits(sink, s_loc)], axis=-1)
        p = jax.nn.softmax(logits, axis=-1)
        return gqa_combine(p[..., :band], vb) + gqa_combine(p[..., band:band + n_ctx], v_ctx)

    ob = lax.map(one_block, (qb, jnp.arange(nb)))
    return jnp.moveaxis(ob, 0, 1).reshape(b, s, h * dh)

def fourier_mix(u):
    b, l, _ = u.shape
    ug = u.astype(jnp.float32).reshape(b, l, F_GROUPS, F_GROUP_CH)
    f = jnp.fft.fftn(ug, axes=(1, 3), norm='ortho').real
    return f.reshape(b, l, F_W).astype(u.dtype)

def mixer_inputs(h, w_in, q_norm, k_norm, rope):
    b, l, _ = h.shape
    widths = (Q_A_W, KV_A_W, KV_A_W, F_W, Q_C_W, KV_C_W, KV_C_W)
    points = [int(p) for p in np.cumsum(widths)[:-1]]
    qa, ka, va, fb, qc, kc, vc = jnp.split(h @ w_in, points, axis=-1)
    qa = rms_norm(qa.reshape(b, l, A_Q_HEADS, HEAD_DIM), q_norm)
    ka = rms_norm(ka.reshape(b, l, A_KV_HEADS, HEAD_DIM), k_norm)
    va = va.reshape(b, l, A_KV_HEADS, HEAD_DIM)
    qc = qc.reshape(b, l, C_Q_HEADS, HEAD_DIM)
    kc = kc.reshape(b, l, C_KV_HEADS, HEAD_DIM)
    vc = vc.reshape(b, l, C_KV_HEADS, HEAD_DIM)
    if rope is not None:
        cos, sin = rope
        qa, ka = apply_rope(qa, cos, sin), apply_rope(ka, cos, sin)
        qc, kc = apply_rope(qc, cos, sin), apply_rope(kc, cos, sin)
    return qa, ka, va, fb, qc, kc, vc

def swiglu(h, w_gate, w_up, w_down):
    return (jax.nn.silu(h @ w_gate) * (h @ w_up)) @ w_down

def second_inputs(seed: int = 0) -> dict:
    key = jax.random.key(seed)
    ks = jax.random.split(key, 18)
    n = jax.random.normal
    f32 = jnp.float32
    return {
        'x': n(ks[0], (BATCH, SEQ, D_MODEL), f32),
        'c': n(ks[1], (BATCH, D_MODEL), f32),
        'ctx': n(ks[2], (BATCH, CTX_LEN, D_MODEL), f32),
        'c_ctx': n(ks[3], (D_MODEL,), f32),
        'w_ada': 0.02 * n(ks[4], (DEPTH, D_MODEL, 6 * D_MODEL), f32),
        'b_ada': 0.01 * n(ks[5], (DEPTH, 6 * D_MODEL), f32),
        'g_mix': 1.0 + 0.05 * n(ks[6], (DEPTH, D_MODEL), f32),
        'g_ffn': 1.0 + 0.05 * n(ks[7], (DEPTH, D_MODEL), f32),
        'w_in': n(ks[8], (DEPTH, D_MODEL, IN_WIDTH), f32) * D_MODEL ** -0.5,
        'q_norm': 1.0 + 0.05 * n(ks[9], (DEPTH, HEAD_DIM), f32),
        'k_norm': 1.0 + 0.05 * n(ks[10], (DEPTH, HEAD_DIM), f32),
        'sink': 0.5 * n(ks[11], (DEPTH, C_Q_HEADS), f32),
        'w_out': n(ks[12], (DEPTH, MIX_WIDTH, D_MODEL), f32) * MIX_WIDTH ** -0.5,
        'w_gate': n(ks[13], (DEPTH, D_MODEL, D_FF), f32) * D_MODEL ** -0.5,
        'w_up': n(ks[14], (DEPTH, D_MODEL, D_FF), f32) * D_MODEL ** -0.5,
        'w_down': n(ks[15], (DEPTH, D_FF, D_MODEL), f32) * D_FF ** -0.5,
        'g_final': 1.0 + 0.05 * n(ks[16], (D_MODEL,), f32),
    }

def second_block(x, c, ctx, c_ctx, w_ada, b_ada, g_mix, g_ffn, w_in, q_norm, k_norm, sink, w_out, w_gate, w_up, w_down, g_final):
    rope = axial_rope_tables(x.shape[1])
    for l in range(DEPTH):
        update_ctx = l < DEPTH - 1
        sh1, sc1, gt1, sh2, sc2, gt2 = [m[:, None, :] for m in adaln(c, w_ada[l], b_ada[l])]
        csh1, csc1, cgt1, csh2, csc2, cgt2 = adaln(c_ctx, w_ada[l], b_ada[l])
        h = rms_norm(x, g_mix[l]) * (1 + sc1) + sh1
        hc = rms_norm(ctx, g_mix[l]) * (1 + csc1) + csh1
        qa, ka, va, fb, qc, kc, vc = mixer_inputs(h, w_in[l], q_norm[l], k_norm[l], rope)
        qac, kac, vac, fbc, qcc, kcc, vcc = mixer_inputs(hc, w_in[l], q_norm[l], k_norm[l], None)
        o = jnp.concatenate([
            global_attention(qa, ka, va, kac, vac),
            fourier_mix(fb),
            window_attention(qc, kc, vc, kcc, vcc, sink[l]),
        ], axis=-1)
        x = x + gt1 * (o @ w_out[l])
        x = x + gt2 * swiglu(rms_norm(x, g_ffn[l]) * (1 + sc2) + sh2, w_gate[l], w_up[l], w_down[l])
        if update_ctx:
            oc = jnp.concatenate([
                dense_attention(qac, kac, vac),
                fourier_mix(fbc),
                dense_attention(qcc, kcc, vcc, sink[l]),
            ], axis=-1)
            ctx = ctx + cgt1 * (oc @ w_out[l])
            ctx = ctx + cgt2 * swiglu(rms_norm(ctx, g_ffn[l]) * (1 + csc2) + csh2, w_gate[l], w_up[l], w_down[l])
    return rms_norm(x, g_final)


def setup_inputs(seed=0):
    out = dict(first_inputs(seed))
    for name, value in second_inputs(seed + 1).items():
        if name != "x":
            out[name + "_2"] = value
    return out


def reference(
    x, mem, positions, w_in, lambda_q1, lambda_k1, lambda_q2, lambda_k2, diff_subln_g, conv_w,
    w_mem_kv, w_br_attn, w_br_conv, w_br_mem, w_out, ln1_g, ln1_b, ln2_g, ln2_b, w_router,
    router_bias, w_exp_gate, w_exp_up, w_exp_down, c_2, ctx_2, c_ctx_2, w_ada_2, b_ada_2,
    g_mix_2, g_ffn_2, w_in_2, q_norm_2, k_norm_2, sink_2, w_out_2, w_gate_2, w_up_2, w_down_2,
    g_final_2,
):
    x = first_block(
        x, mem, positions, w_in, lambda_q1, lambda_k1, lambda_q2, lambda_k2, diff_subln_g,
        conv_w, w_mem_kv, w_br_attn, w_br_conv, w_br_mem, w_out, ln1_g, ln1_b, ln2_g, ln2_b,
        w_router, router_bias, w_exp_gate, w_exp_up, w_exp_down,
    )
    return second_block(
        x, c_2, ctx_2, c_ctx_2, w_ada_2, b_ada_2, g_mix_2, g_ffn_2, w_in_2, q_norm_2, k_norm_2,
        sink_2, w_out_2, w_gate_2, w_up_2, w_down_2, g_final_2,
    )


_drawn_inputs = setup_inputs


def setup_inputs(seed=0):
    import zlib

    import numpy as np

    out = dict(_drawn_inputs(seed))
    spreads = {}
    factors = {'mem': 3.428,
     'lambda_q1': 8.0,
     'lambda_k1': 2.909,
     'lambda_q2': 6.58,
     'lambda_k2': 6.841,
     'diff_subln_g': 8.0,
     'w_mem_kv': 3.347,
     'w_br_mem': 3.481,
     'router_bias': 8.0,
     'b_ada_2': 3.621,
     'g_mix_2': 4.895,
     'q_norm_2': 8.0,
     'k_norm_2': 8.0,
     'sink_2': 8.0}
    for name, (base, spread) in spreads.items():
        noise = np.random.default_rng([zlib.crc32(name.encode()), seed]).standard_normal(out[name].shape)
        drawn = base * np.exp(spread * noise) if base else spread * noise
        out[name] = __import__('jax').numpy.asarray(drawn.astype(out[name].dtype))
    for name, factor in factors.items():
        out[name] = (out[name] * factor).astype(out[name].dtype)
    return out
```

```python
from contextlib import ExitStack, contextmanager

import math

import concourse.bass as bass
from concourse import mybir

ALU = mybir.AluOpType
ACT = mybir.ActivationFunctionType
F32 = mybir.dt.float32
I32 = mybir.dt.int32
AX_X = mybir.AxisListType.X

P = 128
D = 1024
DC = D // P
T = 256
TC = T // P
DEPTH = 2
HEADS = 8
MEM_HEADS = 4
CONV = 512
CC = CONV // P
TAPS = 3
EXPERTS = 16
PER_GROUP = 4
FF1 = 512
FF2 = 2816
FC2 = FF2 // P
SLOTS = 64
PAIRS = EXPERTS // 2
RING = 6
TILE = 4096
HALF = T * D // P // 2
NEG = -1e30
ADA_TILES = 6 * D // 512
ADA_EARLY = 6
ALPHA = float((2 * DEPTH) ** 0.25)
LN_EPS = 1e-5
RMS_EPS = 1e-5
NORM_EPS = 1e-6
PI = math.pi
PI_BELOW = 3.1415925
TWO_PI = (6.28125, 0.00193500518798828125, 2 * math.pi - 6.28125 - 0.00193500518798828125)
ROUNDER = 1.5 * 2.0 ** 23
LAMBDA_INIT = [0.8 - 0.6 * math.exp(-0.3 * l) for l in range(DEPTH)]
PARAM_DMAS = 25
OVER_INC = {"full_act": PAIRS // 2 + 6 * PAIRS, "read_act": PAIRS // 2 + 5 * PAIRS,
            "full_dve": 5 * PAIRS, "read_dve": 5 * PAIRS}

LOOP_STEPS = {'act layer': {'centred': 2,
               'full_act': 294,
               'gates_used': 2,
               'heads': 1,
               'logit_max': 1,
               'max': 24,
               'rounds': 1,
               'scaled': 16,
               'var': 6},
 'act over pair': {'full_act': 6},
 'act pair': {'full_act': 6},
 'act round': {'full_act': 52},
 'dve layer': {'branch_gate': 3,
               'exp': 24,
               'full_dve': 258,
               'gate_copied': 1,
               'logit_exp': 1,
               'norm': 16,
               'scores': 24,
               'sig': 32,
               'sqrt': 6},
 'dve over pair': {'full_dve': 5, 'sig': 1},
 'dve pair': {'full_dve': 5, 'sig': 1},
 'dve round': {'full_dve': 40, 'sig': 8},
 'pe layer': {'attn_out': 1,
              'chosen': 1,
              'conv': 1,
              'exp': 24,
              'gate_read': 32,
              'loaded0': 224,
              'loaded1': 224,
              'loaded2': 224,
              'loaded3': 224,
              'loaded4': 224,
              'loaded5': 224,
              'merged': 1,
              'norm': 16,
              'probs': 24,
              'read_act': 262,
              'read_dve': 258,
              'rounds': 1,
              'select': 4,
              'square': 20},
 'pe over pair': {'gate_read': 1, 'read_act': 5, 'read_dve': 5},
 'pe pair': {'gate_read': 1,
             'loaded0': 16,
             'loaded1': 16,
             'loaded2': 16,
             'loaded3': 16,
             'loaded4': 16,
             'loaded5': 16,
             'read_act': 5,
             'read_dve': 5},
 'pe round': {'gate_read': 8, 'read_act': 44, 'read_dve': 40, 'select': 1},
 'sp layer': {'free': 84, 'rounds': 1},
 'sp pair': {'free': 6}}
FOUND_STEPS = {}


class Counts:

    def __init__(self, engine):
        self.engine, self.k, self.loops = engine, {}, []

    def value(self, name):
        v = self.k.get(name, 0)
        for var, steps in self.loops:
            if steps.get(name, 0):
                v = var * steps[name] + v
        return v

    def next(self, name, n=1):
        self.k[name] = self.k.get(name, 0) + n
        return self.value(name)

    @contextmanager
    def loop(self, eng, n, name):
        key = f"{self.engine} {name}"
        steps = LOOP_STEPS.get(key, {})
        before = dict(self.k)
        with eng.Fori(0, n) as i:
            self.loops.append((i, steps))
            yield i
            self.loops.pop()
        found = {s: v - before.get(s, 0) for s, v in self.k.items() if v != before.get(s, 0)}
        FOUND_STEPS[key] = found
        for s, v in found.items():
            self.k[s] = before.get(s, 0) + n * v


def ds(i, n):
    return bass.ds(i, n)


def build(nc, a, out):
    ctx = ExitStack()
    with ctx:
        def sb(name, shape, dt=F32):
            return ctx.enter_context(nc.sbuf_tensor(name, shape, dt))

        def sem(name):
            return ctx.enter_context(nc.semaphore(name))

        s_inputs = sem("inputs_loaded")
        s_params = sem("params_loaded")
        s_consts = sem("pool_consts_ready")
        s_ones = sem("vector_consts_ready")
        s_loaded = [sem(f"slot{i}_loaded") for i in range(RING)]
        s_free = sem("slots_free")
        s_full = {"act": sem("psum_full_for_act"), "dve": sem("psum_full_for_dve")}
        s_read = {"act": sem("psum_read_by_act"), "dve": sem("psum_read_by_dve")}
        s_cond = sem("cond_ready")
        s_lam = sem("lambda_sums_ready")
        s_lam_exp = sem("lambda_exps_ready")
        s_angle = sem("angles_ready")
        s_tables = sem("rope_tables_ready")
        s_scores = sem("scores_full")
        s_max = sem("row_max_ready")
        s_exp = sem("exp_done")
        s_probs = sem("probs_ready")
        s_gate_copied = sem("conv_gate_copied")
        s_conv = sem("conv_ready")
        s_branch_gate = sem("branch_gates_ready")
        s_gates_used = sem("branch_gates_used")
        s_merged = sem("merged_ready")
        s_heads = sem("heads_ready")
        s_centred = sem("centred_ready")
        s_square = sem("squares_ready")
        s_var = sem("variance_ready")
        s_sqrt = sem("root_ready")
        s_scaled = sem("normalised_ready")
        s_norm = sem("norm_out_ready")
        s_attn_out = sem("attention_scaled")
        s_logit_max = sem("logit_max_ready")
        s_logit_exp = sem("logit_exp_ready")
        s_chosen = sem("expert_choice_ready")
        s_select = sem("selection_ready")
        s_rounds = sem("rounds_ready")
        s_sig = sem("sigmoid_ready")
        s_gate_read = sem("gate_product_read")
        s_ff_read = sem("ff_gate_read")
        s_raw = sem("raw_chunks_copied")
        s_rope = sem("rope_done")
        s_block2 = sem("memory_tokens_done")
        s_tables2 = sem("second_tables_loaded")
        s_final = sem("out_tile_ready")
        s_out = sem("out_written")
        s_settled = sem("settled")
        o_loaded = sem("overflow_weights_loaded")
        o_used = sem("overflow_weights_used")

        ring = sb("ring", [P, RING, TILE])
        X = sb("X", [P, DC, 2 * T])
        memT = sb("memT", [P, DC, T])
        AR = sb("arena", [P, 17700])
        ident = sb("ident", [P, P])
        ones = sb("ones", [P, P])
        mean_d = sb("mean_d", [P, P])
        mean_v = sb("mean_v", [P, P])
        mean_h = sb("mean_h", [P, P])
        before = sb("before", [P, P])
        causal = sb("causal", [P, P])
        behind = sb("behind", [P, P])
        cosT = sb("cosT", [P, T])
        sinT = sb("sinT", [P, T])
        vecA = sb("vecA", [P, 104])
        vecB = sb("vecB", [P, 96])
        vecC = sb("vecC", [P, 46])
        ada = sb("ada", [P, DEPTH, 48, 2])
        cond = sb("cond", [P, DC, 32])
        wr = sb("wr", [P, DC, EXPERTS])
        rbias = sb("rbias", [1, EXPERTS])
        slot_no = sb("slot_no", [P, SLOTS])
        expert_key = sb("expert_key", [P, EXPERTS])
        sinks = sb("sinks", [P, 2 * 6])
        invf = sb("invf", [P, 1])
        picks = sb("picks", [P, 2])
        neglam = sb("neglam", [P, DEPTH])
        subg = sb("subg", [P, DEPTH])
        qk_norm = sb("qk_norm", [P, 2, DEPTH])
        gmod = sb("gmod", [P, DC, 2])
        tiny = sb("tiny", [P, 64])
        rounds_i = sb("rounds_i", [1, 1], I32)

        def view(start, *shape):
            n = 1
            for s in shape:
                n *= s
            v = AR[:, start:start + n]
            if len(shape) == 2:
                v = v.rearrange("p (a b) -> p a b", a=shape[0])
            elif len(shape) == 3:
                v = v.rearrange("p (a b c) -> p a b c", a=shape[0], b=shape[1])
            return v

        raw = {n: view(2048 * i, TC, D) for i, n in enumerate(("x", "mem", "ctx_2"))}
        stackA, stackB, stackC = (view(6144 + P * i, P) for i in range(3))
        lamrows = view(6528, 4, DEPTH, 64)
        lamsum = view(7040, 4)
        pos_i = view(7100, T).bitcast(I32)
        ang = view(7400, 6, T)
        qT, kT = view(0, HEADS, T), view(2048, HEADS, T)
        vtok = view(4096, TC, D)
        cbT = qmT = view(6144, CC, T)
        ccT = kmT = view(7168, CC, T)
        zT = view(8192, CC, T + TAPS - 1)
        vmem = view(8192, TC, CONV)
        gT = view(9224, DC, T)
        oT = view(11272, HEADS, T)
        ymT = view(13320, MEM_HEADS, T)
        mergedT = view(14344, DC, T)
        probs1 = view(16392, 2, 512)
        probT1 = [view(17416, 2 * P), view(9224, 2 * P)]
        tmp1, tmp2 = view(16392, T), view(16648, T)
        part = view(13320, 512)
        res1 = view(0, DC, T)
        sq1 = view(2048, DC, T)
        root1 = view(4096, T)
        xtok = view(0, TC, D)
        sel = view(2048, TC, EXPERTS, SLOTS)
        selg = view(4096, TC, EXPERTS, SLOTS)
        selT = view(6144, PAIRS, T)
        acc = view(8192, DC, T)
        xg = view(10240, DC, P)
        sig1 = view(11264, FF1)
        hid = view(11776, FF1)
        hidT = view(12288, FF1 // P, P)
        yex = view(12800, D)
        rt = view(13848, 16, TC * EXPERTS)
        onehot = [view(14360, TC, EXPERTS), view(14392, TC, EXPERTS)]
        position = view(14424, TC, EXPERTS)
        gatew = view(14456, TC, EXPERTS)
        h2 = view(0, DC, 2 * T)
        pj = view(4096, 12, 2 * T)
        kswap = view(10240, 2, 2 * T)
        vt2 = view(11264, 2, 4, P)
        probs2 = view(12288, 2, 512)
        probT2 = [view(13312, 4 * P), view(13824, 4 * P)]
        root2 = view(13824, 2 * T)
        squares_h = view(11264, 4, 2 * T)
        four = view(14336, 4 * T)
        tmp3, tmp4 = view(15360, T), view(15616, T)
        sq2 = view(4096, DC, 2 * T)
        ff = view(4096, FC2, 2 * T)
        sig2 = view(15360, 2, 2 * T)
        out_tok = view(4096, TC, D)
        dftL = memT[:, 0:4, :]
        dftC = memT[:, 4, :]
        cos2, sin2 = memT[:, 5, :], memT[:, 6, :]

        bank = [ctx.enter_context(nc.psum_tensor(f"bank{i}", [P, 512], F32)) for i in range(8)]
        block = ctx.enter_context(nc.Block())

        def lncol(which, l, c, n=1):
            return vecA[:, ds(16 * which + 8 * l + c, n)]

        def settle(eng):
            eng.sem_inc(s_settled, 1)

        @block.sync
        def _(sp):
            C = Counts("sp")
            for n in ("x", "mem", "ctx_2"):
                sp.dma_start(raw[n], a[n].rearrange("(c p) d -> p c d", p=P)).then_inc(s_inputs, 16)
            sp.sem_inc(s_free, RING)
            sp.wait_ge(s_params, PARAM_DMAS * 16)
            at = [0]

            def tile(src, cols=None, parts=None):
                s = at[0] % RING
                at[0] += 1
                sp.wait_ge(s_free, C.next("free"))
                shape = src.shape
                dst = ring[:, s, 0:shape[1] * shape[2]].rearrange("p (k n) -> p k n", k=shape[1])
                sp.dma_start(dst, src).then_inc(s_loaded[s], 16)

            def rows(w, c0, n):
                return w.rearrange("(k p) n -> p k n", p=P)[:, :, c0:c0 + n]

            def of_layer(name, l):
                return a[name][ds(l, 1)].rearrange("a k n -> (a k) n")

            with C.loop(sp, DEPTH, "layer") as l:
                w = of_layer("w_in", l)
                for c in (0, 1, 2, 3, 4, 5, 6, 7, 8, 12, 13):
                    tile(rows(w, 512 * c, 512))
                tile(rows(of_layer("w_br_conv", l), 0, D))
                for c in (0, 1):
                    tile(rows(of_layer("w_mem_kv", l), 512 * c, 512))
                for c in (9, 14, 15):
                    tile(rows(w, 512 * c, 512))
                tile(rows(of_layer("w_br_mem", l), 0, D))
                for c in range(ADA_EARLY):
                    tile(rows(of_layer("w_ada_2", l), 512 * c, 512))
                for c in (10, 11):
                    tile(rows(w, 512 * c, 512))
                for name in ("w_br_attn", "w_out"):
                    for c in (0, 1):
                        tile(rows(of_layer(name, l), 512 * c, 512))
                for c in range(ADA_EARLY, ADA_TILES):
                    tile(rows(of_layer("w_ada_2", l), 512 * c, 512))
                with C.loop(sp, PAIRS, "pair") as pr:
                    for name in ("w_exp_gate", "w_exp_up", "w_exp_down"):
                        for e in range(2):
                            src = a[name].rearrange("l e k n -> (l e) k n")[ds(l * EXPERTS + pr * 2 + e, 1)]
                            tile(src.rearrange("a (k p) n -> p (a k) n", p=P))
                sp.wait_ge(s_rounds, C.next("rounds"))
                settle(sp)
                more = sp.value_load(rounds_i[0:1, 0:1])
                with sp.Fori(1, T // SLOTS) as rd:
                    with sp.If(more >= rd):
                        sp.wait_ge(s_free, C.value("free") + RING)
                        settle(sp)
                        with sp.Fori(0, PAIRS) as pr:
                            base = (l * (T // SLOTS - 1) + rd - 1) * PAIRS + pr
                            for i, name in enumerate(("w_exp_gate", "w_exp_up", "w_exp_down")):
                                for e in range(2):
                                    src = a[name].rearrange("l e k n -> (l e) k n")[ds(l * EXPERTS + pr * 2 + e, 1)]
                                    src = src.rearrange("a (k p) n -> p (a k) n", p=P)
                                    dst = ring[:, 2 * i + e, :].rearrange("p (k n) -> p k n", k=src.shape[1])
                                    sp.dma_start(dst, src).then_inc(o_loaded, 16)
                            sp.wait_ge(o_loaded, base * 96 + 96)
                            settle(sp)
                            sp.wait_ge(o_used, base + 1)
                            settle(sp)
                    with sp.Else():
                        sp.sem_inc(o_loaded, 96 * PAIRS)
            sp.wait_ge(s_block2, 1)
            sp.dma_start(dftL, a["dft_tokens"]).then_inc(s_tables2, 16)
            sp.dma_start(memT[:, 4:7, :], a["dft_channels_rope"]).then_inc(s_tables2, 16)
            for l in range(DEPTH):
                for c in range(4):
                    tile(rows(a["w_in_2"][l], 384 * c, 384))
                for c in range(2):
                    tile(rows(a["w_out_2"][l], 512 * c, 512))
                for c in range(6):
                    n = min(512, FF2 - 512 * c)
                    tile(rows(a["w_gate_2"][l], 512 * c, n))
                    tile(rows(a["w_up_2"][l], 512 * c, n))
                wd = a["w_down_2"][l].rearrange("(k p) n -> p k n", p=P)
                for half in range(2):
                    for k0 in range(0, FC2, 8):
                        tile(wd[:, k0:min(k0 + 8, FC2), 512 * half:512 * half + 512])
            for n in range(TC):
                sp.wait_ge(s_final, n + 1)
                sp.dma_start(out[P * n:P * n + P, :], view(4096 + D * n, D)).then_inc(s_out, 16)
            sp.wait_ge(s_out, 16 * TC)

        @block.gpsimd
        def _(pool):
            g = nc.gpsimd
            for m, v in ((ident, 0.0), (before, 1.0), (causal, 0.0), (behind, 0.0), (mean_h, 1.0 / 64)):
                g.memset(m[:], v)
            g.memset(picks[:], 0.0)
            g.drain()
            g.affine_select(out=ident[:], in_=ident[:], compare_op=ALU.not_equal, fill=1.0, base=0,
                            pattern=[[-1, P]], channel_multiplier=1)
            g.affine_select(out=before[:], in_=before[:], compare_op=ALU.is_gt, fill=0.0, base=0,
                            pattern=[[1, P]], channel_multiplier=-1)
            g.affine_select(out=causal[:], in_=causal[:], compare_op=ALU.is_ge, fill=NEG, base=0,
                            pattern=[[-1, P]], channel_multiplier=1)
            g.affine_select(out=behind[:], in_=behind[:], compare_op=ALU.is_ge, fill=NEG, base=0,
                            pattern=[[1, P]], channel_multiplier=-1)
            g.drain()
            g.memset(mean_h[0:64, 64:128], 0.0)
            g.memset(mean_h[64:128, 0:64], 0.0)
            g.drain()
            for i in range(2):
                for j in range(4):
                    g.drain()
                    g.affine_select(out=picks[:, i:i + 1], in_=picks[:, i:i + 1], compare_op=ALU.not_equal, fill=1.0,
                                    base=-(32 * j + i), pattern=[[0, 1]], channel_multiplier=1)
            g.iota(slot_no[:], pattern=[[1, SLOTS]], base=0, channel_multiplier=0,
                   allow_small_or_imprecise_dtypes=True)
            g.iota(expert_key[:], pattern=[[-1, EXPERTS]], base=EXPERTS, channel_multiplier=0,
                   allow_small_or_imprecise_dtypes=True)
            g.drain()
            g.memset(tiny[:, 63:64], 0.0).then_inc(s_consts, 1)

        sel2, selg2 = view(2048, TC, PAIRS * P), view(4096, TC, PAIRS * P)
        MEM_BANKS, DIFF_BANKS = [(4,), (5,)], [(4, 5), (2, 3)]
        N_OVER = T // SLOTS - 1

        def tokens2(l):
            return 2 * T if l < DEPTH - 1 else T

        def proj_tokens(l, n):
            return 2 * T if n in (3, 4, 10, 11) else tokens2(l)

        def units2(l):
            us = []
            for kind in (0, 1):
                for h in range(6):
                    for qb in range(TC):
                        us.append((kind, h, qb, 0, 4))
                    if tokens2(l) > T:
                        for qb in range(TC, 2 * TC):
                            us.append((kind, h, qb, TC, 2))
            return us

        @block.tensor
        def _(pe):
            C = Counts("pe")
            last = {}
            at = [0]
            mm = nc.tensor.matmul
            turn = {"act": 0, "dve": 0}

            def free(b):
                if b in last:
                    pe.wait_ge(*last.pop(b))

            def full(ins, b, who):
                ins.then_inc(s_full[who], 1)
                last[b] = (s_read[who], C.next("read_" + who))

            def wait_read(who):
                pe.wait_ge(s_read[who], C.value("read_" + who))

            def all_read():
                wait_read("act")
                wait_read("dve")
                settle(pe)
                last.clear()

            def ring_bank(who):
                b = (0 if who == "act" else 2) + turn[who] % 2
                turn[who] += 1
                free(b)
                return b

            def next_tile():
                s = at[0] % RING
                at[0] += 1
                pe.wait_ge(s_loaded[s], C.next(f"loaded{s}", 16))
                return s

            def used(n=1):
                pe.drain().then_inc(s_free, n)

            def slot(s, k, n):
                return ring[:, s, 0:k * n].rearrange("p (k n) -> p k n", k=k)

            def feature_product(w, chunk, src, nt, who, kc=DC, normed=False):
                b = ring_bank(who)
                for k in range(kc):
                    if normed:
                        pe.wait_ge(s_norm, C.next("norm"))
                    ins = mm(bank[b][:, 0:nt], w[:, k, chunk * P:chunk * P + P], src[:, k, 0:nt],
                             start=(k == 0), stop=(k == kc - 1))
                full(ins, b, who)

            def tile_features(src, nt, who, kc=DC, width=512):
                s = next_tile()
                for c in range(width // P):
                    feature_product(slot(s, kc, width), c, src, nt, who, kc)
                used()

            def token_product(src):
                s = next_tile()
                w = slot(s, DC, 512)
                for tc in range(TC):
                    b = ring_bank("act")
                    for k in range(DC):
                        ins = mm(bank[b][:], src[:, k, tc * P:tc * P + P], w[:, k, :],
                                 start=(k == 0), stop=(k == DC - 1))
                    full(ins, b, "act")
                used()

            def transposes(srcs, b, who):
                free(b)
                for i, s_ in enumerate(srcs):
                    ins = nc.tensor.transpose(bank[b][:, i * P:i * P + P], s_, ident[:])
                full(ins, b, who)

            def run_attention(units, score_banks, between=()):
                held = {}
                copied = {}

                def scores(u):
                    i = u % 2
                    for b in score_banks[i]:
                        free(b)
                    if i in held:
                        pe.wait_ge(s_exp, held.pop(i))
                    units[u]["scores"](score_banks[i]).then_inc(s_scores, 1)
                    held[i] = C.next("exp")

                for s in range(len(units) + 3):
                    if s < len(units):
                        scores(s)
                    if s < len(between):
                        between[s][0]()
                    if 0 <= s - 2 < len(units):
                        un = units[s - 2]
                        pe.wait_ge(s_probs, C.next("probs"))
                        transposes([un["probs"][:, k * P:k * P + P] for k in range(un["n"])], 6, "act")
                        copied[s - 2] = last[6]
                    if 0 <= s - 3 < len(units):
                        un = units[s - 3]
                        pe.wait_ge(*copied.pop(s - 3))
                        free(7)
                        for k in range(un["n"]):
                            ins = mm(bank[7][un["rows"], 0:P], un["values"](k), un["probT"][:, k * P:k * P + P],
                                     start=(k == 0), stop=(k == un["n"] - 1))
                        full(ins, 7, "dve")
                    if s < len(between):
                        between[s][1]()
                for v in held.values():
                    pe.wait_ge(s_exp, v)

            def norm_sums(chunks, nt, mat, b, each=None):
                free(b)
                for c, ch in enumerate(chunks):
                    if each:
                        pe.wait_ge(each, C.next("square"))
                    ins = mm(bank[b][:, 0:nt], mat[:], ch, start=(c == 0), stop=(c == len(chunks) - 1))
                full(ins, b, "dve")

            def sum_step(chunk, c, nt, b):
                if c == 0:
                    free(b)
                ins = mm(bank[b][:, 0:nt], mean_d[:], chunk, start=(c == 0), stop=(c == DC - 1))
                if c == DC - 1:
                    full(ins, b, "dve")

            def square_step(squares, c, nt, b):
                pe.wait_ge(s_square, C.next("square"))
                sum_step(squares[:, c, 0:nt], c, nt, b)

            def variance_sums():
                norm_sums([sq1[:, c, :] for c in range(DC)], T, mean_d, 5, s_square)

            def selections():
                pe.wait_ge(s_select, C.next("select"))
                for p2 in range(0, PAIRS, 2):
                    b = ring_bank("act")
                    for q in range(2):
                        for tc in range(TC):
                            ins = nc.tensor.transpose(bank[b][:, q * T + tc * P:q * T + tc * P + P],
                                                      selg2[:, tc, (p2 + q) * P:(p2 + q) * P + P], ident[:])
                    full(ins, b, "act")
                all_read()

            def expert_pair(pr, take, done):
                for hb in range(2):
                    b = 2 + hb
                    free(b)
                    for c in range(4):
                        ch = 4 * hb + c
                        for tc in range(TC):
                            ins = mm(bank[b][:, c * P:c * P + P], xtok[:, tc, ch * P:ch * P + P],
                                     sel2[:, tc, ds(pr * P, P)], start=(tc == 0), stop=(tc == TC - 1))
                    full(ins, b, "act")
                wait_read("act")
                for b, i in ((0, 0), (1, 2)):
                    free(b)
                    w = [slot(take(i + e), DC, FF1) for e in range(2)]
                    for k in range(DC):
                        for e in range(2):
                            ins = mm(bank[b][64 * e:64 * e + 64, :], xg[:, k, 64 * e:64 * e + 64], w[e][:, k, :],
                                     start=(k == 0), stop=(k == DC - 1))
                    if b == 0:
                        ins.then_inc(s_full["act"], 1)
                        last[0] = (s_gate_read, C.next("gate_read"))
                    else:
                        full(ins, b, "dve")
                    done(2)
                wait_read("dve")
                transposes([hid[:, c * P:c * P + P] for c in range(FF1 // P)], 4, "act")
                wait_read("act")
                w = [slot(take(4 + e), FF1 // P, D) for e in range(2)]
                for nh in range(2):
                    b = 5 + nh
                    free(b)
                    for k in range(FF1 // P):
                        for e in range(2):
                            ins = mm(bank[b][64 * e:64 * e + 64, :], hidT[:, k, 64 * e:64 * e + 64],
                                     w[e][:, k, nh * 512:nh * 512 + 512], start=(k == 0), stop=(k == FF1 // P - 1))
                    full(ins, b, "act")
                done(2)
                wait_read("act")
                for i in range(DC // 2):
                    b = (7, 4)[i % 2]
                    free(b)
                    for cc in range(2):
                        ins = mm(bank[b][:, cc * T:cc * T + T], yex[:, (2 * i + cc) * P:(2 * i + cc) * P + P],
                                 selT[:, ds(pr, 1), :].rearrange("p a t -> p (a t)"), start=True, stop=True)
                    full(ins, b, "dve")
                pe.wait_ge(*last.pop(0))
                all_read()

            pe.wait_ge(s_consts, 1)
            pe.wait_ge(s_ones, 1)
            pe.wait_ge(s_inputs, 48)
            pe.wait_ge(s_params, PARAM_DMAS * 16)
            for n in ("x", "mem", "ctx_2"):
                for c in range(0, DC, 2):
                    b = ring_bank("act")
                    for cc in range(2):
                        for tc in range(TC):
                            ins = nc.tensor.transpose(bank[b][:, cc * T + tc * P:cc * T + tc * P + P],
                                                      raw[n][:, tc, (c + cc) * P:(c + cc) * P + P], ident[:])
                    full(ins, b, "act")
            b = ring_bank("dve")
            nc.tensor.transpose(bank[b][:, 0:104], stackA[0:104, :], ident[0:104, 0:104])
            nc.tensor.transpose(bank[b][:, 128:224], stackB[0:96, :], ident[0:96, 0:96])
            full(nc.tensor.transpose(bank[b][:, 256:302], stackC[0:46, :], ident[0:46, 0:46]), b, "dve")
            ring_bank("dve")
            all_read()
            pe.wait_ge(s_cond, 1)
            pe.wait_ge(s_tables, 1)

            with C.loop(pe, DEPTH, "layer") as l:
                all_read()
                for t in range(4):
                    tile_features(X, T, "dve")
                token_product(X)
                token_product(X)
                tile_features(X, T, "act")
                tile_features(X, T, "act")
                tile_features(X, T, "dve")
                tile_features(X, T, "act")
                tile_features(X, T, "act")
                pe.wait_ge(s_conv, C.next("conv"))
                tile_features(cbT, T, "dve", kc=CC, width=D)
                tile_features(memT, T, "act")
                token_product(memT)
                tile_features(X, T, "act")
                all_read()
                units = []
                for h in range(MEM_HEADS):
                    for blk in range(TC):
                        def sc(bs, h=h, blk=blk):
                            return mm(bank[bs[0]][:, 0:T], qmT[:, h, blk * P:blk * P + P], kmT[:, h, :],
                                      start=True, stop=True)
                        units.append(dict(scores=sc, probs=probs1[:, len(units) % 2, :], n=TC, rows=slice(0, P),
                                          values=lambda k, h=h: vmem[:, k, h * P:h * P + P], probT=probT1[len(units) % 2]))
                run_attention(units, MEM_BANKS)
                wait_read("dve")
                tile_features(X, T, "act")
                tile_features(X, T, "act")
                tile_features(ymT, T, "dve", kc=CC, width=D)
                all_read()
                def partial_sums():
                    w = slot(next_tile(), DC, 512)
                    free(0)
                    for k in range(DC):
                        g = k % 4
                        ins = mm(bank[0][32 * g:32 * g + 32, :], cond[:, k, :], w[:, k, :],
                                 start=(k < 4), stop=(k >= 4))
                    full(ins, 0, "act")
                    used()

                def fold():
                    wait_read("act")
                    free(1)
                    for c in range(4):
                        ins = mm(bank[1][:, 2 * c:2 * c + 2], part[:, c * P:c * P + P], picks[:],
                                 start=True, stop=True)
                    full(ins, 1, "dve")

                units = []
                for h in range(HEADS):
                    for blk in range(TC):
                        def sc(bs, h=h, blk=blk):
                            for c in range(2):
                                ins = mm(bank[bs[c]][:, 0:P * (blk + 1)],
                                         qT[64 * c:64 * c + 64, h, blk * P:blk * P + P],
                                         kT[64 * c:64 * c + 64, h, 0:P * (blk + 1)], start=True, stop=True)
                            return ins
                        units.append(dict(scores=sc, probs=probs1[:, len(units) % 2, :], n=blk + 1, rows=slice(0, P),
                                          values=lambda k, h=h: vtok[:, k, h * P:h * P + P], probT=probT1[len(units) % 2]))
                run_attention(units, DIFF_BANKS, [(partial_sums, fold)] * ADA_EARLY)
                for hp in range(HEADS // 2):
                    norm_sums([view(2048 + 512 * hp, 512)], 512, mean_v, 4 + hp % 2, s_square)
                tile_features(X, T, "act")
                tile_features(X, T, "act")
                pe.wait_ge(s_attn_out, C.next("attn_out"))
                tile_features(oT, T, "dve")
                tile_features(oT, T, "dve")
                pe.wait_ge(s_merged, C.next("merged"))
                written = []
                for t in range(2):
                    w = slot(next_tile(), DC, 512)
                    for c in range(4):
                        feature_product(w, c, mergedT, T, "dve")
                        written.append(last[2 + (turn["dve"] - 1) % 2])
                        if len(written) > 1:
                            pe.wait_ge(*written[-2])
                            sum_step(res1[:, len(written) - 2, :], len(written) - 2, T, 4)
                    used()
                pe.wait_ge(*written[-1])
                sum_step(res1[:, DC - 1, :], DC - 1, T, 4)
                partial_sums()
                fold()
                variance_sums()
                for t in range(2):
                    partial_sums()
                    fold()
                for i in range(4):
                    tc, c0 = divmod(4 * i, DC)
                    if i < 2:
                        pe.wait_ge(s_norm, C.next("norm", 4))
                    transposes([X[:, c0 + j, tc * P:tc * P + P] for j in range(4)], ring_bank("act"), "act")
                free(4)
                for tc in range(TC):
                    o_ = bank[4][:, tc * EXPERTS:(tc + 1) * EXPERTS]
                    for k in range(DC):
                        mm(o_, X[:, k, tc * P:tc * P + P], wr[:, k, :], start=(k == 0), stop=False)
                    ins = mm(o_, ones[0:1, :], rbias[0:1, :], start=False, stop=True)
                full(ins, 4, "dve")
                for t in range(2):
                    partial_sums()
                    fold()
                pe.wait_ge(s_chosen, C.next("chosen"))
                free(5)
                mm(bank[5][:, 0:16], before[:], onehot[0][:, 0, :], start=True, stop=True)
                mm(bank[5][:, 16:32], ones[:], onehot[0][:, 0, :], start=True, stop=False)
                mm(bank[5][:, 16:32], before[:], onehot[0][:, 1, :], start=False, stop=True)
                mm(bank[5][:, 32:48], ones[:], onehot[0][:, 0, :], start=True, stop=False)
                full(mm(bank[5][:, 32:48], ones[:], onehot[0][:, 1, :], start=False, stop=True), 5, "dve")
                partial_sums()
                fold()
                selections()
                with C.loop(pe, PAIRS, "pair") as pr:
                    expert_pair(pr, lambda i: next_tile(), used)
                pe.wait_ge(s_rounds, C.next("rounds"))
                settle(pe)
                more = pe.value_load(rounds_i[0:1, 0:1])
                with C.loop(pe, N_OVER, "round") as rd:
                    with pe.If(more >= rd + 1):
                        selections()
                        with C.loop(pe, PAIRS, "over pair") as pr:
                            pe.wait_ge(o_loaded, ((l * N_OVER + rd) * PAIRS + pr) * 96 + 96)
                            expert_pair(pr, lambda i: i, lambda n: None)
                            pe.drain().then_inc(o_used, 1)
                    with pe.Else():
                        pe.drain().then_inc(o_used, PAIRS)
                        pe.sem_inc(s_full["act"], OVER_INC["full_act"])
                        pe.sem_inc(s_full["dve"], OVER_INC["full_dve"])
                wait_read("dve")
                for c in range(DC):
                    sum_step(acc[:, c, :], c, T, 4)
                variance_sums()
                pe.wait_ge(s_norm, C.next("norm", DC))
                all_read()
            pe.drain().then_inc(s_block2, 1)
            pe.wait_ge(s_tables2, 32)

            for c in range(DC):
                square_step(h2, c, 2 * T, 0)
            for l in range(DEPTH):
                nt = tokens2(l)
                for t in range(4):
                    w = slot(next_tile(), DC, 384)
                    for c in range(3):
                        feature_product(w, c, h2, proj_tokens(l, 3 * t + c), "act", normed=(t + c == 0))
                    used()
                    if t == 1:
                        for n in range(4):
                            norm_sums([squares_h[:, n, 0:proj_tokens(l, n)]], proj_tokens(l, n), mean_h, 4 + n % 2,
                                      s_square)
                wait_read("dve")
                wait_read("act")
                for j, n in enumerate((4, 11)):
                    transposes([pj[:, n, tc * P:tc * P + P] for tc in range(4)], ring_bank("act"), "act")
                for i in range(nt // T):
                    for g in range(2):
                        for tc in range(TC):
                            b = ring_bank("act")
                            full(mm(bank[b][:, 0:T], pj[:, 5 + g, i * T + tc * P:i * T + tc * P + P], dftC,
                                    start=True, stop=True), b, "act")
                    wait_read("act")
                    for g in range(2):
                        b = ring_bank("dve")
                        for tc in range(TC):
                            for s_ in range(2):
                                f0 = (2 * g + tc) * T + s_ * P
                                ins = mm(bank[b][:, 0:T], four[:, f0:f0 + P], dftL[:, 2 * s_ + tc, :],
                                         start=(tc + s_ == 0), stop=(tc + s_ == 2))
                        full(ins, b, "dve")
                pe.wait_ge(s_rope, C.next("rope"))
                wait_read("act")
                units = []
                for kind, h, qb, k0, n in units2(l):
                    par, kv = h % 2, h // 3
                    def sc(bs, kind=kind, h=h, qb=qb, k0=k0, n=n, par=par, kv=kv):
                        q = pj[:, (0, 7)[kind] + h // 2, qb * P:qb * P + P]
                        keys = pj[:, (3, 10)[kind], :] if par == kv else kswap[:, kind, :]
                        r = slice(64 * par, 64 * par + 64)
                        return mm(bank[bs[0]][:, 0:n * P], q[r], keys[r, k0 * P:(k0 + n) * P], start=True, stop=True)
                    units.append(dict(scores=sc, probs=probs2[:, len(units) % 2, :], n=n, probT=probT2[len(units) % 2],
                                      rows=slice(64 * par, 64 * par + 64),
                                      values=lambda k, kind=kind, kv=kv, k0=k0:
                                      vt2[:, kind, k0 + k, 64 * kv:64 * kv + 64]))
                run_attention(units, MEM_BANKS)
                wait_read("dve")
                for t in range(2):
                    w = slot(next_tile(), DC, 512)
                    for c in range(4):
                        feature_product(w, c, h2, nt, "dve")
                        if t + c:
                            square_step(sq2, 4 * t + c - 1, nt, 4)
                    used()
                square_step(sq2, DC - 1, nt, 4)
                for t in range(6):
                    width = min(512, FF2 - 512 * t)
                    wg, wu = (slot(next_tile(), DC, width) for _ in range(2))
                    for c in range(width // P):
                        b = ring_bank("act")
                        for k in range(DC):
                            if t + c == 0:
                                pe.wait_ge(s_norm, C.next("norm"))
                            ins = mm(bank[b][:, 0:nt], wg[:, k, c * P:c * P + P], h2[:, k, 0:nt],
                                     start=(k == 0), stop=(k == DC - 1))
                        ins.then_inc(s_full["act"], 1)
                        last[b] = (s_ff_read, C.next("ff_read"))
                        feature_product(wu, c, h2, nt, "dve")
                    used(2)
                wait_read("dve")
                for half in range(2):
                    for c in range(4):
                        free(4 + c)
                    for k0 in range(0, FC2, 8):
                        kn = min(8, FC2 - k0)
                        w = slot(next_tile(), kn, 512)
                        for k in range(kn):
                            for c in range(4):
                                ins = mm(bank[4 + c][:, 0:nt], w[:, k, c * P:c * P + P], ff[:, k0 + k, 0:nt],
                                         start=(k0 + k == 0), stop=(k0 + k == FC2 - 1))
                                if k0 + k == FC2 - 1:
                                    full(ins, 4 + c, "dve")
                        used()
                        if half and k0 == 0:
                            for c in range(4):
                                square_step(h2, c, nt, 0)
                for c in range(4, DC):
                    square_step(h2, c, nt, 0)
            pe.wait_ge(s_norm, C.next("norm", DC))
            for i in range(4):
                tc, c0 = divmod(4 * i, DC)
                transposes([h2[:, c0 + j, tc * P:tc * P + P] for j in range(4)], ring_bank("act"), "act")
            all_read()

        @block.scalar
        def _(act):
            C = Counts("act")
            turn = [0]
            fn = nc.scalar.activation

            rows = [(stackA, 16 * i, 16, a[n].rearrange("l (c p) -> (l c) p", p=P)) for i, n in
                    enumerate(("ln1_g", "ln1_b", "ln2_g", "ln2_b", "g_mix_2", "g_ffn_2"))]
            rows.append((stackA, 96, 8, a["g_final_2"].rearrange("(c p) -> c p", p=P)))
            rows.append((stackB, 0, 96, a["b_ada_2"].rearrange("l (c p) -> (l c) p", p=P)))
            rows.append((stackC, 0, 24, a["conv_w"].rearrange("l t (c p) -> (l t c) p", p=P)))
            rows.append((stackC, 24, 2, a["diff_subln_g"]))
            rows.append((stackC, 26, 8, a["c_2"].rearrange("a (c p) -> (a c) p", p=P)))
            rows.append((stackC, 34, 8, a["c_ctx_2"].rearrange("(c p) -> c p", p=P)))
            for st, r0, n, src in rows:
                act.dma_start(st[r0:r0 + n, :], src).then_inc(s_params, 16)
            for i, n in enumerate(("q_norm_2", "k_norm_2")):
                for half in range(2):
                    act.dma_start(stackC[42 + 2 * i:44 + 2 * i, 64 * half:64 * half + 64], a[n]).then_inc(s_params, 16)
            for i, n in enumerate(("lambda_q1", "lambda_k1", "lambda_q2", "lambda_k2")):
                act.dma_start(lamrows[:, i, :, :], a[n].partition_broadcast(P)).then_inc(s_params, 16)
            act.dma_start(pos_i, a["positions"][0, :].partition_broadcast(P)).then_inc(s_params, 16)
            act.dma_start(sinks[:], a["sink_2"].rearrange("l h -> (l h)").partition_broadcast(P)).then_inc(s_params, 16)
            act.dma_start(wr[:], a["w_router"].rearrange("(k p) n -> p k n", p=P)).then_inc(s_params, 16)
            act.dma_start(rbias[:], a["router_bias"].rearrange("(o n) -> o n", o=1)).then_inc(s_params, 16)
            act.dma_start(invf[:], a["inv_freq"]).then_inc(s_params, 16)
            assert len(rows) + 4 + 4 + 5 == PARAM_DMAS

            def take():
                act.wait_ge(s_full["act"], C.next("full_act"))
                b = turn[0] % 2
                turn[0] += 1
                return bank[b]

            def done(ins):
                ins.then_inc(s_read["act"], 1)

            def copy_chunk(dst, n=T, func=ACT.Copy, scale=1.0):
                done(fn(dst, take()[:, 0:n], func, scale=scale))

            def run_attention(units, between=0):
                def exps(u):
                    un = units[u]
                    act.wait_ge(s_max, C.next("max"))
                    o = 8 * (u % 2)
                    for i, b in enumerate(un["banks"][u % 2]):
                        ins = fn(un["probs"][:, i * 256:i * 256 + un["n"] * P], bank[b][:, 0:un["n"] * P], ACT.Exp,
                                 bias=tiny[:, o + i:o + i + 1], accum_out=tiny[:, o + 2 + i:o + 3 + i])
                    if un.get("sink") is not None:
                        ins = fn(tiny[:, o + 5:o + 6], un["sink"], ACT.Exp, bias=tiny[:, o:o + 1])
                    ins.then_inc(s_exp, 1)

                for s in range(len(units) + 2):
                    if s < between:
                        act.wait_ge(s_full["act"], C.next("full_act"))
                        done(nc.scalar.copy(part, bank[0][:]))
                    if 0 <= s - 2:
                        un = units[s - 2]
                        act.wait_ge(s_full["act"], C.next("full_act"))
                        done(nc.scalar.copy(un["probT"][:, 0:un["n"] * P], bank[6][:, 0:un["n"] * P]))
                    if s < len(units):
                        exps(s)

            def squares(chunks):
                for dst, src in chunks:
                    fn(dst, src, ACT.Square).then_inc(s_square, 1)

            def root(dst):
                act.wait_ge(s_var, C.next("var"))
                fn(dst, dst, ACT.Sqrt).then_inc(s_sqrt, 1)

            def partial_sum():
                act.wait_ge(s_full["act"], C.next("full_act"))
                done(nc.scalar.copy(part, bank[0][:]))

            def layer_norm(src, which, l, between=(0, 0)):
                for _ in range(between[0]):
                    partial_sum()
                act.wait_ge(s_centred, C.next("centred"))
                squares([(sq1[:, c, :], src[:, c, :]) for c in range(DC)])
                for _ in range(between[1]):
                    partial_sum()
                root(root1)
                for c in range(DC):
                    act.wait_ge(s_scaled, C.next("scaled"))
                    fn(X[:, c, 0:T], src[:, c, :], ACT.Identity, scale=lncol(which, l, c), bias=lncol(which + 1, l, c)) \
                        .then_inc(s_norm, 1)

            def selections():
                for p2 in range(0, PAIRS, 2):
                    copy_chunk(selT[:, p2:p2 + 2, :].rearrange("p a t -> p (a t)"), 2 * T)

            def expert_pair():
                for hb in range(2):
                    act.wait_ge(s_full["act"], C.next("full_act"))
                    done(nc.scalar.copy(xg[:, 4 * hb:4 * hb + 4, :], bank[2 + hb][:].rearrange("p (c s) -> p c s", c=4)))
                act.wait_ge(s_full["act"], C.next("full_act"))
                fn(sig1, bank[0][:], ACT.Sigmoid).then_inc(s_sig, 1)
                act.wait_ge(s_full["act"], C.next("full_act"))
                done(nc.scalar.copy(hidT.rearrange("p a b -> p (a b)"), bank[4][:]))
                for nh in range(2):
                    act.wait_ge(s_full["act"], C.next("full_act"))
                    done(nc.scalar.copy(yex[:, 512 * nh:512 * nh + 512], bank[5 + nh][:]))

            for dst, t0 in ((X, 0), (memT, 0), (X, T)):
                for c in range(0, DC, 2):
                    done(nc.scalar.copy(dst[:, c:c + 2, t0:t0 + T], take()[:].rearrange("p (c t) -> p c t", c=2)))
            act.wait_ge(s_lam, 1)
            fn(lamsum, lamsum, ACT.Exp).then_inc(s_lam_exp, 1)
            fn(tiny[:, 16:32], tiny[:, 0:16], ACT.Sigmoid).then_inc(s_lam_exp, 1)
            act.wait_ge(s_angle, 1)
            fn(cosT[:], ang[:, 1, :], ACT.Sin).then_inc(s_angle, 1)
            fn(sinT[:], ang[:, 0, :], ACT.Sin).then_inc(s_angle, 1)

            with C.loop(act, DEPTH, "layer") as l:
                for half in range(2):
                    for tc in range(TC):
                        copy_chunk(vtok[:, tc, 512 * half:512 * half + 512], 512)
                for dst in (cbT, ccT):
                    for c in range(CC):
                        copy_chunk(dst[:, c, :])
                act.drain().then_inc(s_gate_copied, 1)
                for c in range(DC):
                    copy_chunk(gT[:, c, :], func=ACT.Sigmoid)
                act.drain().then_inc(s_branch_gate, 1)
                for c in range(CC):
                    copy_chunk(kmT[:, c, :])
                for tc in range(TC):
                    copy_chunk(vmem[:, tc, :], 512)
                for c in range(MEM_HEADS):
                    copy_chunk(qmT[:, c, :], scale=float(P) ** -0.5)
                run_attention([dict(banks=MEM_BANKS, probs=probs1[:, u % 2, :], n=TC, probT=probT1[u % 2])
                               for u in range(MEM_HEADS * TC)])
                act.wait_ge(s_gates_used, C.next("gates_used"))
                for c in range(DC):
                    copy_chunk(gT[:, c, :], func=ACT.Sigmoid)
                act.drain().then_inc(s_branch_gate, 1)
                run_attention([dict(banks=DIFF_BANKS, probs=probs1[:, u % 2, :], n=u % 2 + 1, probT=probT1[u % 2])
                               for u in range(HEADS * TC)], ADA_EARLY)
                act.wait_ge(s_heads, C.next("heads"))
                heads = [(view(2048 + 512 * i, 512), oT[:, 2 * i:2 * i + 2, :].rearrange("p a t -> p (a t)"))
                         for i in range(HEADS // 2)]
                squares(heads)
                for v, _ in heads:
                    root(v)
                act.wait_ge(s_gates_used, C.next("gates_used"))
                for c in range(DC):
                    copy_chunk(gT[:, c, :], func=ACT.Sigmoid)
                act.drain().then_inc(s_branch_gate, 1)
                layer_norm(res1, 0, l, between=(1, 2))
                act.drain()
                for i in range(4):
                    copy_chunk(xtok[:, i // 2, 512 * (i % 2):512 * (i % 2) + 512], 512)
                act.wait_ge(s_logit_max, C.next("logit_max"))
                for tc in range(TC):
                    ins = fn(rt[:, 1, tc * EXPERTS:(tc + 1) * EXPERTS], rt[:, 0, tc * EXPERTS:(tc + 1) * EXPERTS],
                             ACT.Exp, bias=tiny[:, tc:tc + 1])
                ins.then_inc(s_logit_exp, 1)
                for _ in range(3):
                    partial_sum()
                selections()
                with C.loop(act, PAIRS, "pair"):
                    expert_pair()
                act.wait_ge(s_rounds, C.next("rounds"))
                settle(act)
                more = act.value_load(rounds_i[0:1, 0:1])
                with C.loop(act, N_OVER, "round") as rd:
                    with act.If(more >= rd + 1):
                        selections()
                        with C.loop(act, PAIRS, "over pair"):
                            expert_pair()
                    with act.Else():
                        act.drain().then_inc(s_sig, PAIRS)
                        act.sem_inc(s_read["act"], OVER_INC["read_act"])
                layer_norm(acc, 2, l)

            def squares2(dst, nt, wait):
                for c in range(DC):
                    if wait:
                        act.wait_ge(s_scaled, C.next("scaled"))
                    fn(dst[:, c, 0:nt], X[:, c, 0:nt], ACT.Square).then_inc(s_square, 1)

            def modulate(nt, shift):
                root(root2[:, 0:nt])
                for c in range(DC):
                    act.wait_ge(s_scaled, C.next("scaled"))
                    for j in range(nt // T):
                        ins = fn(h2[:, c, j * T:j * T + T], h2[:, c, j * T:j * T + T], ACT.Identity,
                                 scale=gmod[:, c, j:j + 1], bias=shift(c, j))
                    ins.then_inc(s_norm, 1)

            act.drain()
            squares2(h2, 2 * T, False)
            for l in range(DEPTH):
                nt = tokens2(l)
                modulate(2 * T, lambda c, j: ada[:, l, c, j:j + 1])

                def raw_copy(n):
                    copy_chunk(pj[:, n, 0:proj_tokens(l, n)], proj_tokens(l, n), scale=0.125 if n in (7, 8, 9) else 1.0)

                for n in range(4):
                    raw_copy(n)
                act.drain()
                for n in range(4):
                    m = proj_tokens(l, n)
                    fn(squares_h[:, n, 0:m], pj[:, n, 0:m], ACT.Square).then_inc(s_square, 1)
                for n in range(4, 8):
                    raw_copy(n)
                for n in range(4):
                    root(squares_h[:, n, 0:proj_tokens(l, n)])
                for n in range(8, 12):
                    raw_copy(n)
                act.drain().then_inc(s_raw, 1)
                for j in range(2):
                    if j == 0:
                        act.wait_ge(s_scaled, C.next("scaled"))
                    copy_chunk(vt2[:, j, :, :].rearrange("p a b -> p (a b)"), 512)
                for i in range(nt // T):
                    for g in range(2):
                        for tc in range(TC):
                            copy_chunk(four[:, (2 * g + tc) * T:(2 * g + tc + 1) * T])
                us = units2(l)
                run_attention([dict(banks=MEM_BANKS, probs=probs2[:, u % 2, :], n=n, probT=probT2[u % 2],
                                    sink=sinks[:, 6 * l + h:6 * l + h + 1] if kind else None)
                               for u, (kind, h, qb, k0, n) in enumerate(us)])
                squares2(sq2, nt, True)
                modulate(nt, lambda c, j: ada[:, l, 24 + c, j:j + 1])
                for i in range(FC2):
                    b = take()
                    if i >= 2:
                        act.wait_ge(s_ff_read, C.next("ff_read"))
                    fn(sig2[:, i % 2, 0:nt], b[:, 0:nt], ACT.Sigmoid).then_inc(s_sig, 1)
                act.wait_ge(s_ff_read, C.next("ff_read", 2))
                squares2(h2, nt, True)
            root(root2[:, 0:T])
            for i in range(4):
                copy_chunk(out_tok[:, i // 2, 512 * (i % 2):512 * (i % 2) + 512], 512)
                if i % 2:
                    act.drain().then_inc(s_final, 1)

        @block.vector
        def _(dve):
            C = Counts("dve")
            turn = [0]
            v = nc.vector
            tt, tsc, stt, drain = v.tensor_tensor, v.tensor_scalar, v.scalar_tensor_tensor, v.drain

            def take():
                dve.wait_ge(s_full["dve"], C.next("full_dve"))
                b = 2 + turn[0] % 2
                turn[0] += 1
                return bank[b]

            def filled():
                dve.wait_ge(s_full["dve"], C.next("full_dve"))

            def done(ins):
                ins.then_inc(s_read["dve"], 1)

            def quads(dst, src, sines):
                for q in range(4):
                    i, o = slice(32 * q, 32 * q + 32), slice(32 * (q ^ 1), 32 * (q ^ 1) + 32)
                    ins = tt(dst[o], src[i], sines[i], ALU.mult)
                return ins

            def run_attention(units, between=()):
                def maxima(u):
                    un = units[u]
                    dve.wait_ge(s_scores, C.next("scores"))
                    o, n, bs = 8 * (u % 2), un["n"] * P, un["banks"][u % 2]
                    if un.get("mask") is not None:
                        m, c0 = un["mask"]
                        for b in bs:
                            tt(bank[b][:, c0:c0 + P], bank[b][:, c0:c0 + P], m[:], ALU.add)
                        drain()
                    for i, b in enumerate(bs):
                        ins = v.tensor_reduce(tiny[:, o + i:o + i + 1], bank[b][:, 0:n], AX_X, ALU.max, negate=True)
                    if un.get("sink") is not None:
                        drain()
                        stt(tiny[:, o + 4:o + 5], un["sink"], -1.0, tiny[:, o:o + 1], ALU.mult, ALU.min)
                        drain()
                        ins = v.tensor_copy(tiny[:, o:o + 1], tiny[:, o + 4:o + 5])
                    ins.then_inc(s_max, 1)

                def normalise(u):
                    un = units[u]
                    dve.wait_ge(s_exp, C.next("exp"))
                    o, n, p_ = 8 * (u % 2), un["n"] * P, un["probs"]
                    if un.get("sink") is not None:
                        tt(tiny[:, o + 2:o + 3], tiny[:, o + 2:o + 3], tiny[:, o + 5:o + 6], ALU.add)
                        drain()
                    if un.get("minus") is not None:
                        v.reciprocal(tiny[:, o + 4:o + 6], tiny[:, o + 2:o + 4])
                        drain()
                        tt(tiny[:, o + 6:o + 7], tiny[:, o + 5:o + 6], un["minus"], ALU.mult)
                        tsc(p_[:, 0:n], p_[:, 0:n], tiny[:, o + 4:o + 5], None, ALU.mult)
                        drain()
                        stt(p_[:, 0:n], p_[:, 256:256 + n], tiny[:, o + 6:o + 7], p_[:, 0:n], ALU.mult, ALU.add) \
                            .then_inc(s_probs, 1)
                    else:
                        v.reciprocal(tiny[:, o + 4:o + 5], tiny[:, o + 2:o + 3])
                        drain()
                        tsc(p_[:, 0:n], p_[:, 0:n], tiny[:, o + 4:o + 5], None, ALU.mult).then_inc(s_probs, 1)

                def outputs(u):
                    filled()
                    done(v.tensor_copy(units[u]["out"], bank[7][units[u]["rows"], 0:P]))

                for s in range(len(units) + 3):
                    if s < len(units):
                        maxima(s)
                    if 0 <= s - 1 < len(units):
                        normalise(s - 1)
                    if 0 <= s - 3:
                        outputs(s - 3)
                    if s < len(between):
                        between[s]()

            def variance(b, dst, eps, w):
                filled()
                done(tsc(dst, bank[b][:, 0:w], eps, None, ALU.add))
                drain().then_inc(s_var, 1)

            def inverse(dst):
                dve.wait_ge(s_sqrt, C.next("sqrt"))
                v.reciprocal(dst, dst)
                drain()

            def layer_norm(src, between=(0, 0), of=None):
                filled()
                done(tt(src, src, bank[4][:, 0:T].unsqueeze(1).to_broadcast([P, DC, T]), ALU.subtract))
                drain().then_inc(s_centred, 1)
                for t in range(between[0]):
                    of(ADA_EARLY + t)()
                variance(5, root1, LN_EPS, T)
                for t in range(between[1]):
                    of(ADA_EARLY + between[0] + t)()
                inverse(root1)
                for c in range(DC):
                    tt(src[:, c, :], src[:, c, :], root1, ALU.mult).then_inc(s_scaled, 1)
                dve.wait_ge(s_norm, C.next("norm", DC))

            def selections():
                for tc in range(TC):
                    tt(sel[:, tc, :, :], slot_no[:].unsqueeze(1).to_broadcast([P, EXPERTS, SLOTS]),
                       position[:, tc, :].unsqueeze(2).to_broadcast([P, EXPERTS, SLOTS]), ALU.is_equal)
                drain()
                for tc in range(TC):
                    tt(selg[:, tc, :, :], sel[:, tc, :, :],
                       gatew[:, tc, :].unsqueeze(2).to_broadcast([P, EXPERTS, SLOTS]), ALU.mult)
                drain().then_inc(s_select, 1)

            def expert_pair():
                dve.wait_ge(s_sig, C.next("sig"))
                tt(hid, sig1, bank[0][:], ALU.mult).then_inc(s_gate_read, 1)
                drain()
                filled()
                done(tt(hid, hid, bank[1][:], ALU.mult))
                for i in range(DC // 2):
                    filled()
                    b = bank[(7, 4)[i % 2]]
                    done(tt(acc[:, 2 * i:2 * i + 2, :], acc[:, 2 * i:2 * i + 2, :],
                            b[:].rearrange("p (c t) -> p c t", c=2), ALU.add))

            for m, x_ in ((ones, 1.0), (mean_d, 1.0 / D), (mean_v, 1.0 / P), (cond, 0.0)):
                v.memset(m[:], x_)
            drain().then_inc(s_ones, 1)
            b = take()
            v.tensor_copy(vecA[:], b[:, 0:104])
            v.tensor_copy(vecB[:], b[:, 128:224])
            done(v.tensor_copy(vecC[:], b[:, 256:302]))
            turn[0] += 1
            drain()
            for i in range(2):
                tt(lamrows[:, 2 * i, :, :], lamrows[:, 2 * i, :, :], lamrows[:, 2 * i + 1, :, :], ALU.mult)
            v.tensor_copy(tiny[:, 0:16], vecC[:, 26:42])
            drain()
            for i in range(2):
                v.tensor_reduce(lamsum[:, 2 * i:2 * i + 2], lamrows[:, 2 * i, :, :], AX_X, ALU.add)
            drain().then_inc(s_lam, 1)
            dve.wait_ge(s_lam_exp, 2)
            for l in range(DEPTH):
                tsc(neglam[:, l:l + 1], lamsum[:, 2 + l:3 + l], lamsum[:, l:l + 1], -LAMBDA_INIT[l],
                    ALU.subtract, ALU.add)
                tsc(subg[:, l:l + 1], vecC[:, 24 + l:25 + l], 1.0 - LAMBDA_INIT[l], None, ALU.mult)
            for j in range(2):
                tt(cond[:, :, j], tiny[:, 8 * j:8 * j + 8], tiny[:, 16 + 8 * j:24 + 8 * j], ALU.mult)
            for l in range(DEPTH):
                tsc(qk_norm[:, 0, l:l + 1], vecC[:, 42 + l:43 + l], 0.125, None, ALU.mult)
                v.tensor_copy(qk_norm[:, 1, l:l + 1], vecC[:, 44 + l:45 + l])
            drain().then_inc(s_cond, 1)
            v.tensor_copy(ang[:, 2, :], pos_i)
            drain()
            tsc(ang[:, 0, :], ang[:, 2, :], invf[:], None, ALU.mult)
            drain()
            tsc(ang[:, 3, :], ang[:, 0, :], 1.0 / (2 * PI), None, ALU.mult)
            drain()
            tsc(ang[:, 4, :], ang[:, 3, :], ROUNDER, None, ALU.add)
            drain()
            tsc(ang[:, 3, :], ang[:, 4, :], -ROUNDER, None, ALU.add)
            drain()
            for part_ in TWO_PI:
                stt(ang[:, 0, :], ang[:, 3, :], -part_, ang[:, 0, :], ALU.mult, ALU.add)
                drain()
            tsc(ang[:, 0, :], ang[:, 0, :], PI_BELOW, -PI_BELOW, ALU.min, ALU.max)
            drain()
            tsc(ang[:, 1, :], ang[:, 0, :], PI / 2, None, ALU.add)
            drain()
            tsc(ang[:, 4, :], ang[:, 1, :], PI, -2 * PI, ALU.is_gt, ALU.mult)
            drain()
            tt(ang[:, 1, :], ang[:, 1, :], ang[:, 4, :], ALU.add)
            drain()
            tsc(ang[:, 1, :], ang[:, 1, :], PI_BELOW, -PI_BELOW, ALU.min, ALU.max)
            drain().then_inc(s_angle, 1)
            dve.wait_ge(s_angle, 3)
            for q in (1, 3):
                tsc(sinT[32 * q:32 * q + 32, :], sinT[32 * q:32 * q + 32, :], -1.0, None, ALU.mult)
            drain().then_inc(s_tables, 1)

            with C.loop(dve, DEPTH, "layer") as l:
                for dst, scale in ((qT, 0.125), (kT, 1.0)):
                    for h in range(HEADS):
                        b = take()
                        stt(tmp1, b[:, 0:T], scale, cosT[:], ALU.mult, ALU.mult)
                        for q in range(4):
                            i, o = slice(32 * q, 32 * q + 32), slice(32 * (q ^ 1), 32 * (q ^ 1) + 32)
                            ins = stt(tmp2[o], b[i, 0:T], scale, sinT[i], ALU.mult, ALU.mult)
                        drain()
                        done(tt(dst[:, h, :], tmp1, tmp2, ALU.add))
                        drain()
                v.memset(zT[:, :, 0:TAPS - 1], 0.0)
                dve.wait_ge(s_gate_copied, C.next("gate_copied"))
                for c in range(CC):
                    done(tt(zT[:, c, TAPS - 1:], take()[:, 0:T], ccT[:, c, :], ALU.mult))
                drain()
                w_conv = lambda t, c: vecC[:, ds(l * (TAPS * CC) + t * CC + c, 1)]
                for c in range(CC):
                    tsc(ccT[:, c, :], zT[:, c, 0:T], w_conv(0, c), None, ALU.mult)
                for t in (1, 2):
                    drain()
                    for c in range(CC):
                        stt(ccT[:, c, :], zT[:, c, t:t + T], w_conv(t, c), ccT[:, c, :], ALU.mult, ALU.add)
                drain()
                tt(cbT, cbT, ccT, ALU.mult)
                drain().then_inc(s_conv, 1)
                dve.wait_ge(s_branch_gate, C.next("branch_gate"))
                for c in range(DC):
                    done(tt(mergedT[:, c, :], take()[:, 0:T], gT[:, c, :], ALU.mult))
                drain().then_inc(s_gates_used, 1)
                run_attention([dict(banks=MEM_BANKS, probs=probs1[:, (TC * h + blk) % 2, :], n=TC, rows=slice(0, P),
                                    out=ymT[:, h, blk * P:blk * P + P])
                               for h in range(MEM_HEADS) for blk in range(TC)])

                def merge():
                    dve.wait_ge(s_branch_gate, C.next("branch_gate"))
                    for c in range(DC):
                        done(tt(gT[:, c, :], take()[:, 0:T], gT[:, c, :], ALU.mult))
                    drain()
                    tt(mergedT, mergedT, gT, ALU.add)

                merge()
                drain().then_inc(s_gates_used, 1)
                def conditioning(t):
                    def go():
                        filled()
                        done(tt(ada[:, ds(l, 1), 4 * t:4 * t + 4, :].rearrange("p a c j -> p (a c) j"),
                                bank[1][:, 0:8].rearrange("p (c j) -> p c j", c=4),
                                vecB[:, ds(l * 48 + 4 * t, 4)].unsqueeze(2).to_broadcast([P, 4, 2]), ALU.add))
                    return go

                run_attention([dict(banks=DIFF_BANKS, probs=probs1[:, blk, :], n=blk + 1, rows=slice(0, P),
                                    mask=(causal, blk * P), minus=neglam[:, ds(l, 1)],
                                    out=oT[:, h, blk * P:blk * P + P])
                               for h in range(HEADS) for blk in range(TC)],
                              [conditioning(t) for t in range(ADA_EARLY)])
                drain().then_inc(s_heads, 1)
                heads = [(view(2048 + 512 * i, 512), oT[:, 2 * i:2 * i + 2, :].rearrange("p a t -> p (a t)"))
                         for i in range(HEADS // 2)]
                for i, (r, _) in enumerate(heads):
                    variance(4 + i % 2, r, RMS_EPS, 512)
                for r, o_ in heads:
                    inverse(r)
                    stt(o_, o_, subg[:, ds(l, 1)], r, ALU.mult, ALU.mult)
                drain().then_inc(s_attn_out, 1)
                merge()
                drain().then_inc(s_merged, 1)
                for c in range(DC):
                    done(stt(res1[:, c, :], X[:, c, 0:T], ALPHA, take()[:, 0:T], ALU.mult, ALU.add))
                drain()
                layer_norm(res1, (1, 2), conditioning)
                tsc(acc, X[:, :, 0:T], ALPHA, None, ALU.mult)
                filled()
                both = lambda ap: ap.rearrange("p (a e) -> p a e", a=TC)
                r_ = lambda i: rt[:, i, :]
                t_ = lambda i, n=2: tiny[:, i:i + n]
                wide = lambda ap, n: ap.unsqueeze(2).to_broadcast([P, ap.shape[1], n])
                key = expert_key[:].unsqueeze(1).to_broadcast([P, TC, EXPERTS])
                done(v.tensor_copy(r_(0), bank[4][:, 0:TC * EXPERTS]))
                drain()
                v.tensor_reduce(t_(0), both(r_(0)), AX_X, ALU.max, negate=True)
                drain().then_inc(s_logit_max, 1)
                for t in range(ADA_EARLY + 3, ADA_EARLY + 5):
                    conditioning(t)()
                dve.wait_ge(s_logit_exp, C.next("logit_exp"))
                quad = lambda ap: ap.rearrange("p (g e) -> p g e", e=PER_GROUP)
                v.tensor_reduce(t_(2, 8), quad(r_(1)), AX_X, ALU.max)
                drain()
                v.tensor_reduce(t_(10), both(t_(2, 8)), AX_X, ALU.max)
                drain()
                tt(both(t_(12, 8)), both(t_(2, 8)), wide(t_(10), 4), ALU.is_equal)
                drain()
                tt(both(t_(20, 8)), both(t_(12, 8)), expert_key[:, 12:16].unsqueeze(1).to_broadcast([P, TC, 4]), ALU.mult)
                drain()
                v.tensor_reduce(t_(28), both(t_(20, 8)), AX_X, ALU.max)
                drain()
                tt(both(t_(12, 8)), both(t_(20, 8)), wide(t_(28), 4), ALU.is_equal)
                drain()
                tt(quad(r_(2)), quad(r_(1)), wide(t_(12, 8), PER_GROUP), ALU.mult)
                tsc(t_(40, 8), t_(12, 8), -1.0, None, ALU.add)
                drain()
                tt(quad(r_(2)), quad(r_(2)), wide(t_(40, 8), PER_GROUP), ALU.add)
                drain()
                for i in range(2):
                    v.tensor_reduce(t_(30 + 2 * i), both(r_(2)), AX_X, ALU.max)
                    drain()
                    tt(both(r_(3)), both(r_(2)), wide(t_(30 + 2 * i), EXPERTS), ALU.is_equal)
                    drain()
                    tt(both(r_(4)), both(r_(3)), key, ALU.mult)
                    drain()
                    v.tensor_reduce(t_(36), both(r_(4)), AX_X, ALU.max)
                    drain()
                    tt(both(r_(5 + i)), both(r_(4)), wide(t_(36), EXPERTS), ALU.is_equal)
                    drain()
                    if i == 0:
                        stt(r_(2), r_(5), -4.0, r_(2), ALU.mult, ALU.add)
                        drain()
                flat = lambda ap: ap.rearrange("p a e -> p (a e)")
                tt(flat(onehot[0]), r_(5), r_(6), ALU.add)
                tt(t_(34), t_(30), t_(32), ALU.add)
                drain().then_inc(s_chosen, 1)
                v.reciprocal(t_(34), t_(34))
                drain()
                for i in range(2):
                    tt(t_(48 + 2 * i), t_(30 + 2 * i), t_(34), ALU.mult)
                drain()
                for i in range(2):
                    tt(both(r_(7 + i)), both(r_(5 + i)), wide(t_(48 + 2 * i), EXPERTS), ALU.mult)
                drain()
                tt(flat(gatew), r_(7), r_(8), ALU.add)
                filled()
                stt(flat(position), bank[5][:, 0:32], 1e4, flat(onehot[0]), ALU.add, ALU.mult)
                done(v.tensor_reduce(t_(52, 1), bank[5][:, 32:48], AX_X, ALU.max))
                drain()
                tsc(flat(position), flat(position), -1e4, None, ALU.add)
                for i in range(N_OVER):
                    tsc(t_(53 + i, 1), t_(52, 1), float(SLOTS * (i + 1)), None, ALU.is_gt)
                drain()
                v.tensor_reduce(t_(57, 1), t_(53, N_OVER), AX_X, ALU.add)
                drain()
                v.tensor_copy(rounds_i[:], tiny[0:1, 57:58])
                drain().then_inc(s_rounds, 1)
                conditioning(ADA_EARLY + 5)()
                selections()
                with C.loop(dve, PAIRS, "pair"):
                    expert_pair()
                more = dve.value_load(rounds_i[0:1, 0:1])
                with C.loop(dve, N_OVER, "round") as rd:
                    with dve.If(more >= rd + 1):
                        tsc(flat(position), flat(position), float(-SLOTS), None, ALU.add)
                        drain()
                        selections()
                        with C.loop(dve, PAIRS, "over pair"):
                            expert_pair()
                    with dve.Else():
                        drain().then_inc(s_read["dve"], OVER_INC["read_dve"])
                        dve.sem_inc(s_gate_read, PAIRS)
                        dve.sem_inc(s_select, 1)
                drain()
                layer_norm(acc)

            dve.wait_ge(s_tables2, 32)

            def rms(nt, which, l, scale0, b=0):
                for c in range(DC):
                    if scale0 is not None:
                        tsc(gmod[:, c, :], ada[:, l, scale0 + c, :], 1.0, lncol(which, l, c), ALU.add, ALU.mult)
                variance(b, root2[:, 0:nt], NORM_EPS, nt)
                inverse(root2[:, 0:nt])
                for c in range(DC):
                    if scale0 is not None:
                        tt(h2[:, c, 0:nt], X[:, c, 0:nt], root2[:, 0:nt], ALU.mult).then_inc(s_scaled, 1)
                    else:
                        stt(h2[:, c, 0:nt], X[:, c, 0:nt], lncol(which, 0, c), root2[:, 0:nt], ALU.mult, ALU.mult) \
                            .then_inc(s_norm, 1)

            for l in range(DEPTH):
                nt = tokens2(l)
                rms(2 * T, 4, l, 8)
                for n in range(4):
                    m = proj_tokens(l, n)
                    variance(4 + n % 2, squares_h[:, n, 0:m], NORM_EPS, m)
                for n in range(4):
                    m = proj_tokens(l, n)
                    inverse(squares_h[:, n, 0:m])
                    stt(pj[:, n, 0:m], pj[:, n, 0:m], qk_norm[:, n // 3, l:l + 1], squares_h[:, n, 0:m], ALU.mult, ALU.mult)
                drain().then_inc(s_scaled, 1)
                for n in (0, 1, 2, 3, 7, 8, 9, 10):
                    if n == 7:
                        dve.wait_ge(s_raw, C.next("raw"))
                    tt(tmp3, pj[:, n, 0:T], cos2, ALU.mult)
                    quads(tmp4, pj[:, n, 0:T], sin2)
                    drain()
                    tt(pj[:, n, 0:T], tmp3, tmp4, ALU.add)
                    drain()
                for j, n in enumerate((3, 10)):
                    for q in range(2):
                        v.tensor_copy(kswap[64 * (1 - q):64 * (1 - q) + 64, j, :], pj[64 * q:64 * q + 64, n, :])
                for i in range(nt // T):
                    for g in range(2):
                        done(v.tensor_copy(h2[:, 3 + g, i * T:i * T + T], take()[:, 0:T]))
                drain().then_inc(s_rope, 1)
                units = []
                for u, (kind, h, qb, k0, n) in enumerate(units2(l)):
                    par = h % 2
                    mask = None
                    if kind and qb < TC:
                        mask = ((causal, P), (behind, 0))[qb]
                    r = slice(64 * par, 64 * par + 64)
                    units.append(dict(banks=MEM_BANKS, probs=probs2[:, u % 2, :], n=n, rows=r, mask=mask,
                                      sink=sinks[:, 6 * l + h:6 * l + h + 1] if kind else None,
                                      out=h2[r, (0, 5)[kind] + h // 2, qb * P:qb * P + P]))
                run_attention(units)

                def gated_residual(c, b, g0):
                    for j in range(nt // T):
                        ins = stt(X[:, c, j * T:j * T + T], b[:, j * T:j * T + T], ada[:, l, g0 + c, j:j + 1],
                                  X[:, c, j * T:j * T + T], ALU.mult, ALU.add)
                    done(ins)
                    drain().then_inc(s_scaled, 1)

                for c in range(DC):
                    gated_residual(c, take(), 16)
                rms(nt, 5, l, 32, 4)
                for i in range(FC2):
                    dve.wait_ge(s_sig, C.next("sig"))
                    tt(ff[:, i, 0:nt], sig2[:, i % 2, 0:nt], bank[i % 2][:, 0:nt], ALU.mult).then_inc(s_ff_read, 1)
                    drain()
                    b = take()
                    done(tt(ff[:, i, 0:nt], ff[:, i, 0:nt], b[:, 0:nt], ALU.mult))
                for c in range(DC):
                    filled()
                    gated_residual(c, bank[4 + c % 4], 40)
            rms(T, 6, 0, None)




def _constants(np):
    inv = (10000.0 ** (-np.arange(0, 64, 2, dtype=np.float64) / 64)).astype(np.float32)
    inv_freq = np.tile(inv, 4).reshape(P, 1)
    t = np.arange(T)
    at = 2 * np.pi * (np.outer(t, t) % T) / T
    norm = 1.0 / math.sqrt(T * 64)
    tokens = np.stack([f[c * P:(c + 1) * P] for f in (np.cos(at), -np.sin(at)) for c in range(TC)], axis=1) * norm
    c = np.arange(64)
    ac = 2 * np.pi * (np.outer(c, c) % 64) / 64
    channels = np.zeros((P, 1, 2 * P))
    for g in range(2):
        channels[64 * g:64 * g + 64, 0, 64 * g:64 * g + 64] = np.cos(ac)
        channels[64 * g:64 * g + 64, 0, P + 64 * g:P + 64 * g + 64] = np.sin(ac)
    inv2 = (10000.0 ** (-np.arange(0, 32, 2, dtype=np.float64) / 32)).astype(np.float32)
    row, col = (t // 64).astype(np.float32), (t % 64).astype(np.float32)
    ang = np.concatenate([inv2[:, None] * row, inv2[:, None] * col]).astype(np.float64)
    cos = np.tile(np.cos(ang), (4, 1))[:, None]
    sin = np.concatenate([np.sin(ang), -np.sin(ang)] * 2)[:, None]
    return {"inv_freq": inv_freq, "dft_tokens": tokens.astype(np.float32),
            "dft_channels_rope": np.concatenate([channels, cos, sin], axis=1).astype(np.float32)}


def kernel(**inputs):
    import numpy as np
    import concourse.bacc as bacc
    from concourse.bass_utils import run_bass_kernel_spmd as run

    nc = bacc.Bacc("TRN2", target_bir_lowering=False, num_devices=1)
    shapes = {"x": (T, D), "mem": (T, D), "ctx_2": (T, D)}
    arrays, aps = {}, {}
    for name, value in {**inputs, **_constants(np)}.items():
        value = np.ascontiguousarray(value)
        value = value.reshape(shapes.get(name, value.shape))
        arrays[f"in_{name}"] = value
        aps[name] = nc.dram_tensor(f"in_{name}", value.shape, mybir.dt.from_np(value.dtype), kind="ExternalInput").ap()
    out = nc.dram_tensor("out_x", (T, D), F32, kind="ExternalOutput").ap()
    build(nc, aps, out)
    result = run(nc, [arrays], core_ids=[0])
    return result.results[0]["out_x"].reshape(1, T, D)
```
